# Optimizing a Trainium2 kernel written in Bass

```python
import math
import jax, jax.numpy as jnp
from jax import lax
import numpy as np

D_MODEL = 2048
BATCH = 1
SEQ = 256
DEPTH = 2

N_META = 16
GRID_W = 64
Q_BLOCK = 128
MIX_WIDTH = D_MODEL
BRANCH_W = MIX_WIDTH // 4
EPS = 1e-6
ROPE_THETA = 500000.0
AXIAL_THETA = 10000.0

A_V_DIM = 128
A_HEADS = BRANCH_W // A_V_DIM
A_QK_DIM = A_V_DIM // 2
A_ROT = A_QK_DIM // 4

B_HEAD_DIM = 128
B_HEADS = BRANCH_W // B_HEAD_DIM
B_KV_HEADS = B_HEADS // 2

C_V_DIM = 128
C_HEADS = BRANCH_W // C_V_DIM
C_NOPE = 128
C_ROPE = 64
C_Q_LORA = 3 * D_MODEL // 16
C_KV_LORA = D_MODEL // 8

POOL_WINDOWS = (2, 4, 8, 16)
D_GROUPS = len(POOL_WINDOWS)
D_GROUP_DIM = BRANCH_W // D_GROUPS

IN_SIZES = (
    A_HEADS * 2 * A_QK_DIM,
    A_HEADS * 2 * A_QK_DIM,
    A_HEADS * A_V_DIM,
    BRANCH_W,
    B_HEADS * B_HEAD_DIM,
    B_KV_HEADS * B_HEAD_DIM,
    B_KV_HEADS * B_HEAD_DIM,
    BRANCH_W,
    C_Q_LORA,
    C_KV_LORA,
    C_ROPE,
    BRANCH_W,
    BRANCH_W,
    BRANCH_W,
)
IN_COLS = sum(IN_SIZES)

kernel_name = 'hybrid_parallel_heads_encoder'

def rms_norm(x, w):
    x32 = x.astype(jnp.float32)
    y = x32 * lax.rsqrt(jnp.mean(x32 * x32, axis=-1, keepdims=True) + EPS)
    return (y * w.astype(jnp.float32)).astype(x.dtype)

def rope_table(pos, dim, theta):
    inv = theta ** (-jnp.arange(0, dim, 2, dtype=jnp.float32) / dim)
    ang = pos.astype(jnp.float32)[:, None] * inv[None, :]
    return jnp.cos(ang), jnp.sin(ang)

def apply_rope(x, cos, sin):
    half = x.shape[-1] // 2
    x1, x2 = x[..., :half], x[..., half:]
    c = cos.astype(x.dtype)
    s = sin.astype(x.dtype)
    return jnp.concatenate([x1 * c - x2 * s, x1 * s + x2 * c], axis=-1)

def softmax32(s, scale):
    return jax.nn.softmax(s.astype(jnp.float32) * scale, axis=-1)

def over_query_blocks(attend, qs):
    meta = tuple(q[:, :N_META] for q in qs)

    def to_blocks(q):
        b, l = q.shape[:2]
        n = (l - N_META) // Q_BLOCK
        return jnp.moveaxis(q[:, N_META:].reshape(b, n, Q_BLOCK, *q.shape[2:]), 1, 0)

    blocks = tuple(to_blocks(q) for q in qs)
    out = lax.map(lambda qb: attend(*qb), blocks)
    out = jnp.moveaxis(out, 0, 1)
    out = out.reshape(out.shape[0], -1, *out.shape[3:])
    return jnp.concatenate([attend(*meta), out], axis=1)

def diff_attention(q_raw, k_raw, v_raw, q_norm_w, k_norm_w, lam_params, subln_w, lambda_init, cos, sin):
    b, l = q_raw.shape[:2]
    q = rms_norm(q_raw.reshape(b, l, A_HEADS, 2, A_QK_DIM), q_norm_w)
    k = rms_norm(k_raw.reshape(b, l, A_HEADS, 2, A_QK_DIM), k_norm_w)
    c, s = cos[:, None, None, :], sin[:, None, None, :]
    q = jnp.concatenate([apply_rope(q[..., :A_ROT], c, s), q[..., A_ROT:]], axis=-1)
    k = jnp.concatenate([apply_rope(k[..., :A_ROT], c, s), k[..., A_ROT:]], axis=-1)
    v = v_raw.reshape(b, l, A_HEADS, A_V_DIM)
    lp = lam_params.astype(jnp.float32)
    lam = jnp.exp(jnp.sum(lp[0] * lp[1])) - jnp.exp(jnp.sum(lp[2] * lp[3])) + lambda_init
    scale = A_QK_DIM ** -0.5

    def attend(qb):
        p = softmax32(jnp.einsum('bqhmd,bkhmd->bhmqk', qb, k), scale)
        w = (p[:, :, 0] - lam * p[:, :, 1]).astype(v.dtype)
        return jnp.einsum('bhqk,bkhd->bqhd', w, v)

    o = over_query_blocks(attend, (q,))
    o = rms_norm(o, subln_w) * (1.0 - lambda_init)
    return o.reshape(b, l, BRANCH_W)

def axial_gqa(q_raw, k_raw, v_raw, q_norm_w, k_norm_w, cos_r, sin_r, cos_c, sin_c):
    b, l = q_raw.shape[:2]
    q = rms_norm(q_raw.reshape(b, l, B_HEADS, B_HEAD_DIM), q_norm_w)
    k = rms_norm(k_raw.reshape(b, l, B_KV_HEADS, B_HEAD_DIM), k_norm_w)
    v = v_raw.reshape(b, l, B_KV_HEADS, B_HEAD_DIM)
    half = B_HEAD_DIM // 2

    def axial(t):
        return jnp.concatenate([
            apply_rope(t[..., :half], cos_r[:, None, :], sin_r[:, None, :]),
            apply_rope(t[..., half:], cos_c[:, None, :], sin_c[:, None, :])], axis=-1)

    q, k = axial(q), axial(k)
    rep = B_HEADS // B_KV_HEADS
    scale = B_HEAD_DIM ** -0.5

    def attend(qb):
        bq, nq = qb.shape[:2]
        qg = qb.reshape(bq, nq, B_KV_HEADS, rep, B_HEAD_DIM)
        p = softmax32(jnp.einsum('bqgrd,bkgd->bgrqk', qg, k), scale).astype(v.dtype)
        return jnp.einsum('bgrqk,bkgd->bqgrd', p, v).reshape(bq, nq, BRANCH_W)

    return over_query_blocks(attend, (q,))

def latent_attention(cq_raw, ckv_raw, kr_raw, q_lat_w, kv_lat_w, w_uq, w_ukv, q_norm_w, k_norm_w, cos, sin):
    b, l = cq_raw.shape[:2]
    c_q = rms_norm(cq_raw, q_lat_w)
    c_kv = rms_norm(ckv_raw, kv_lat_w)
    q = jnp.einsum('blr,rn->bln', c_q, w_uq).reshape(b, l, C_HEADS, C_NOPE + C_ROPE)
    kv = jnp.einsum('blr,rn->bln', c_kv, w_ukv).reshape(b, l, C_HEADS, C_NOPE + C_V_DIM)
    q_nope = rms_norm(q[..., :C_NOPE], q_norm_w[:C_NOPE])
    q_rope = apply_rope(rms_norm(q[..., C_NOPE:], q_norm_w[C_NOPE:]), cos[:, None, :], sin[:, None, :])
    k_nope = rms_norm(kv[..., :C_NOPE], k_norm_w[:C_NOPE])
    v = kv[..., C_NOPE:]
    k_rope = apply_rope(rms_norm(kr_raw, k_norm_w[C_NOPE:]), cos, sin)
    scale = (C_NOPE + C_ROPE) ** -0.5

    def attend(qn, qr):
        s = (jnp.einsum('bqhd,bkhd->bhqk', qn, k_nope).astype(jnp.float32)
             + jnp.einsum('bqhd,bkd->bhqk', qr, k_rope).astype(jnp.float32))
        p = softmax32(s, scale).astype(v.dtype)
        return jnp.einsum('bhqk,bkhd->bqhd', p, v).reshape(qn.shape[0], qn.shape[1], BRANCH_W)

    return over_query_blocks(attend, (q_nope, q_rope))

def multiscale_pool(u, w_group, scale):
    b, l, _ = u.shape
    u32 = u.astype(jnp.float32)
    cs = jnp.concatenate([jnp.zeros((b, 1, BRANCH_W), jnp.float32), lax.cumsum(u32, axis=1)], axis=1)
    t = jnp.arange(l)
    outs = []
    for g, w in enumerate(POOL_WINDOWS):
        lo = jnp.clip(t - w // 2, 0, l)
        hi = jnp.clip(t + w - w // 2, 0, l)
        sl = slice(g * D_GROUP_DIM, (g + 1) * D_GROUP_DIM)
        csg = cs[..., sl]
        cnt = (hi - lo).astype(jnp.float32)[None, :, None]
        mean = (jnp.take(csg, hi, axis=1) - jnp.take(csg, lo, axis=1)) / cnt
        outs.append(mean - u32[..., sl])
    pooled = jnp.stack(outs, axis=2).astype(u.dtype)
    mixed = jnp.einsum('blgc,gcd->blgd', pooled, w_group).reshape(b, l, BRANCH_W)
    return mixed * scale

def hybrid_layer(x, norm_w, w_in, w_out, a_q_norm, a_k_norm, a_lambda, a_subln, b_q_norm, b_k_norm,
                 c_q_lat_norm, c_kv_lat_norm, c_w_uq, c_w_ukv, c_q_norm, c_k_norm, d_w_group, d_scale,
                 lambda_init, tabs):
    cos_a, sin_a, cos_r, sin_r, cos_c, sin_c, cos_m, sin_m = tabs
    h = rms_norm(x, norm_w)
    proj = jnp.einsum('bld,dn->bln', h, w_in)
    split_points = [int(v) for v in np.cumsum(IN_SIZES)[:-1]]
    (aq, ak, av, ag, bq, bk, bv, bg, cq, ckv, ckr, cg, du, dg) = jnp.split(proj, split_points, axis=-1)
    ya = diff_attention(aq, ak, av, a_q_norm, a_k_norm, a_lambda, a_subln, lambda_init, cos_a, sin_a)
    yb = axial_gqa(bq, bk, bv, b_q_norm, b_k_norm, cos_r, sin_r, cos_c, sin_c)
    yc = latent_attention(cq, ckv, ckr, c_q_lat_norm, c_kv_lat_norm, c_w_uq, c_w_ukv, c_q_norm, c_k_norm, cos_m, sin_m)
    yd = multiscale_pool(du, d_w_group, d_scale)
    y = jnp.concatenate([ya * jax.nn.silu(ag), yb * jax.nn.silu(bg),
                         yc * jax.nn.silu(cg), yd * jax.nn.silu(dg)], axis=-1)
    return x + jnp.einsum('bln,nd->bld', y, w_out)

def setup_inputs(seed: int = 0) -> dict:
    key = jax.random.key(seed)
    ks = jax.random.split(key, 24)
    f32 = jnp.float32

    def nrm(k, shape, scale):
        return jax.random.normal(k, shape, f32) * scale

    def gain(k, shape):
        return 1.0 + 0.02 * jax.random.normal(k, shape, f32)

    return {
        'x': nrm(ks[0], (BATCH, SEQ, D_MODEL), 1.0),
        'meta_tokens': nrm(ks[1], (N_META, D_MODEL), 1.0),
        'norm_w': gain(ks[2], (DEPTH, D_MODEL)),
        'w_in': nrm(ks[3], (DEPTH, D_MODEL, IN_COLS), D_MODEL ** -0.5),
        'w_out': nrm(ks[4], (DEPTH, MIX_WIDTH, D_MODEL), MIX_WIDTH ** -0.5),
        'a_q_norm': gain(ks[5], (DEPTH, A_QK_DIM)),
        'a_k_norm': gain(ks[6], (DEPTH, A_QK_DIM)),
        'a_lambda': nrm(ks[7], (DEPTH, 4, A_QK_DIM), 0.1),
        'a_subln': gain(ks[8], (DEPTH, A_V_DIM)),
        'b_q_norm': gain(ks[9], (DEPTH, B_HEAD_DIM)),
        'b_k_norm': gain(ks[10], (DEPTH, B_HEAD_DIM)),
        'c_q_lat_norm': gain(ks[11], (DEPTH, C_Q_LORA)),
        'c_kv_lat_norm': gain(ks[12], (DEPTH, C_KV_LORA)),
        'c_w_uq': nrm(ks[13], (DEPTH, C_Q_LORA, C_HEADS * (C_NOPE + C_ROPE)), C_Q_LORA ** -0.5),
        'c_w_ukv': nrm(ks[14], (DEPTH, C_KV_LORA, C_HEADS * (C_NOPE + C_V_DIM)), C_KV_LORA ** -0.5),
        'c_q_norm': gain(ks[15], (DEPTH, C_NOPE + C_ROPE)),
        'c_k_norm': gain(ks[16], (DEPTH, C_NOPE + C_ROPE)),
        'd_w_group': nrm(ks[17], (DEPTH, D_GROUPS, D_GROUP_DIM, D_GROUP_DIM), D_GROUP_DIM ** -0.5),
        'd_scale': gain(ks[18], (DEPTH, BRANCH_W)),
    }

def reference(x, meta_tokens, norm_w, w_in, w_out, a_q_norm, a_k_norm, a_lambda, a_subln, b_q_norm, b_k_norm,
              c_q_lat_norm, c_kv_lat_norm, c_w_uq, c_w_ukv, c_q_norm, c_k_norm, d_w_group, d_scale):
    b, n_tok, d = x.shape
    rows = n_tok // GRID_W
    l = N_META + n_tok
    h = jnp.concatenate([jnp.broadcast_to(meta_tokens[None].astype(x.dtype), (b, N_META, d)), x], axis=1)

    pos = jnp.arange(l, dtype=jnp.int32)
    cos_a, sin_a = rope_table(pos, A_ROT, ROPE_THETA)
    cos_m, sin_m = rope_table(pos, C_ROPE, ROPE_THETA)
    row_pos = jnp.concatenate([jnp.full((N_META,), -1, jnp.int32),
                               jnp.repeat(jnp.arange(rows, dtype=jnp.int32), GRID_W)])
    col_pos = jnp.concatenate([jnp.arange(N_META, dtype=jnp.int32),
                               jnp.tile(jnp.arange(GRID_W, dtype=jnp.int32), rows)])
    cos_r, sin_r = rope_table(row_pos, B_HEAD_DIM // 2, AXIAL_THETA)
    cos_c, sin_c = rope_table(col_pos, B_HEAD_DIM // 2, AXIAL_THETA)
    tabs = (cos_a, sin_a, cos_r, sin_r, cos_c, sin_c, cos_m, sin_m)

    for i in range(DEPTH):
        lambda_init = 0.8 - 0.6 * math.exp(-0.3 * i)
        h = hybrid_layer(h, norm_w[i], w_in[i], w_out[i], a_q_norm[i], a_k_norm[i], a_lambda[i], a_subln[i],
                         b_q_norm[i], b_k_norm[i], c_q_lat_norm[i], c_kv_lat_norm[i], c_w_uq[i], c_w_ukv[i],
                         c_q_norm[i], c_k_norm[i], d_w_group[i], d_scale[i], lambda_init, tabs)
    return h[:, N_META:]


_drawn_inputs = setup_inputs


def setup_inputs(seed=0):
    import zlib

    import numpy as np

    out = dict(_drawn_inputs(seed))
    spreads = {}
    factors = {'norm_w': 3.504,
     'a_q_norm': 8.0,
     'a_k_norm': 8.0,
     'a_subln': 30.103,
     'b_q_norm': 8.0,
     'b_k_norm': 8.0,
     'c_q_lat_norm': 8.0,
     'c_kv_lat_norm': 8.0,
     'c_q_norm': 8.0,
     'c_k_norm': 8.0,
     'd_scale': 8.0}
    for name, (base, spread) in spreads.items():
        noise = np.random.default_rng([zlib.crc32(name.encode()), seed]).standard_normal(out[name].shape)
        drawn = base * np.exp(spread * noise) if base else spread * noise
        out[name] = __import__('jax').numpy.asarray(drawn.astype(out[name].dtype))
    for name, factor in factors.items():
        out[name] = (out[name] * factor).astype(out[name].dtype)
    return out
```

```python
import math
from contextlib import ExitStack

import concourse.bass as bass
import numpy as np
from concourse import mybir

D_MODEL, SEQ, DEPTH, N_META, GRID_W = 2048, 256, 2, 16, 64
L = N_META + SEQ
EPS = 1e-6
KT = D_MODEL // 128
CK = 4
CHUNK = CK * 256
N_PAIRS = 23
O_PAIRS = D_MODEL // 256
U_CHUNKS = 5
LEAD_PAIRS = 4
SLOTS = 4 * N_PAIRS + U_CHUNKS + 4 * O_PAIRS
ENTRIES = (SLOTS + 1) // 2
RAW, RING, AHEAD = 3, 4, 3
K_BLOCKS = [(0, 128), (128, 128), (256, L - 256)]

OFF = dict(aq=0, ak=512, av=1024, ag=1536, bq=2048, bk=2560, bv=2816, bg=3072, cq=3584, ckv=3968,
           ckr=4224, cg=4288, du=4800, dg=5312)
PAIRS = [("cq", 0), ("ckv", 0), ("cqr", 2), ("cg", 0), ("cg", 2), ("du", 0), ("du", 2),
         ("aq", 0), ("ak", 0), ("av", 0), ("ag", 0), ("aq", 2), ("ak", 2), ("av", 2), ("ag", 2),
         ("bk", 0), ("bv", 0), ("bq", 0), ("bg", 0), ("bq", 2), ("bg", 2), ("dg", 0), ("dg", 2)]

PC = dict(norm=0, aq=16, ak=17, sub=18, bq=19, bk=20, cq=21, ckv=24, qn=26, qr=27, kn=28, kr=29, dsc=30)
N_PAR = 34
CC = dict(cos_a=0, sin_a=L, cos_b=2 * L, sin_b=3 * L, cos_c=4 * L, sin_c=5 * L, ident=6 * L,
          ones=6 * L + 128, halves=6 * L + 256, swap8=6 * L + 384, swap32=6 * L + 512, edge=6 * L + 640)
N_CONST = 6 * L + 640 + 64


def lambda_init(layer):
    return 0.8 - 0.6 * math.exp(-0.3 * layer)


def pair_slot(p):
    return 4 * p + (U_CHUNKS if p >= LEAD_PAIRS else 0)


def first_query(layer):
    return N_META if layer == DEPTH - 1 else 0


def query_tiles(layer):
    q0 = first_query(layer)
    return [(q, min(128, L - q)) for q in range(q0, L, 128)]


def score_steps(layer):
    n = len(query_tiles(layer))
    first = {("c", 0): pair_slot(5) + 2, ("c", 2): pair_slot(7),
             ("a", 0): pair_slot(10) + 2, ("a", 1): pair_slot(12) + 1, ("a", 2): pair_slot(14) + 2,
             ("a", 3): pair_slot(16) + 1, ("b", 0): pair_slot(18) + 3, ("b", 2): pair_slot(20) + 3}
    return [(s0 + 2 * i, b, h, i) for (b, h), s0 in first.items() for i in range(n)]


def make_plan():
    evac, fin, pre, pe = {}, {}, {}, {}

    def at(table, slot, stage):
        table.setdefault(slot, []).append(stage)

    for l in range(DEPTH):
        g0 = l * SLOTS
        at(pe, g0, ("xsum", l))
        at(fin, g0 + 1, ("xscale", l))
        for p, (kind, i0) in enumerate(PAIRS):
            end = g0 + pair_slot(p) + 3
            at(evac, end + 1, ("evac", l, p, 0))
            at(evac, end + 1, ("evac", l, p, 1))
            for j in (0, 1):
                s = end + 1 + j
                if kind in ("aq", "ak", "bq", "bk"):
                    at(pre, s, ("rope_pre", l, kind, i0 + j, j))
                    at(pe, s, ("rope_stat", l, kind, i0 + j))
                    at(fin, s + 1, ("rope_fin", l, kind, i0 + j))
                elif kind in ("av", "bv"):
                    at(pe, s, ("v_turn", l, kind, i0 + j, j))
                    at(fin, s + 1, ("v_out", l, kind, i0 + j))
                elif kind in ("ag", "bg", "cg", "dg"):
                    at(pre, s, ("gate", l, kind, i0 + j, j))
                elif kind == "du":
                    at(pre, s, ("pool", l, i0 + j, j))
                    at(pe, s + 1, ("mix", l, i0 + j))
                    at(fin, s + 2, ("mix_out", l, i0 + j))
        s = g0 + pair_slot(3)
        for n, key in enumerate(("cq", "ckv")):
            at(pre, s + n, ("lat_pre", l, key))
            at(pe, s + n, ("lat_stat", l, key))
            at(fin, s + n + 1, ("lat_fin", l, key))
        at(pre, s + 2, ("rope_pre", l, "kr", 0, None))
        at(pe, s + 2, ("rope_stat", l, "kr", 0))
        at(fin, s + 3, ("rope_fin", l, "kr", 0))
        s = g0 + pair_slot(3) + 4
        for c in range(U_CHUNKS):
            at(evac, s + c + 1, ("up_out", l, c))
        posts = [("qn", 0), ("kn", 0), ("qr", 0), ("qn", 1), ("kn", 1),
                 ("qn", 2), ("kn", 2), ("qr", 1), ("qn", 3), ("kn", 3)]
        for n, (key, i) in enumerate(posts):
            s = g0 + pair_slot(4) + 1 + n
            at(pre, s, ("rope_pre", l, key, i, None))
            at(pe, s, ("rope_stat", l, key, i))
            at(fin, s + 1, ("rope_fin", l, key, i))
        last = len(query_tiles(l)) - 1
        for n, (s, b, h, i) in enumerate(score_steps(l)):
            s += g0
            at(pe, s, ("score", l, n))
            at(fin, s + 1, ("softmax", l, n))
            at(pe, s + 1, ("p_turn", l, n))
            at(fin, s + 2, ("p_out", l, n))
            at(pe, s + 2, ("pv", l, n))
            if b != "a":
                at(fin, s + 3, ("head_out", l, n))
            elif i == last:
                s += 3
                while any(x[0] in ("rope_stat", "lat_stat", "sub_stat") for x in pe.get(s, [])):
                    s += 1
                at(pre, s, ("sub_pre", l, n))
                at(pe, s, ("sub_stat", l, n))
                at(fin, s + 1, ("sub_fin", l, n))
        for n in range(O_PAIRS):
            at(evac, g0 + pair_slot(N_PAIRS) + 4 * n + 4, ("x_out", l, n))
    first_used = {"score": 3, "pv": 0, "p_turn": 1}
    plan = [("setup", 0)] + [("split", 0, s) for s in range(AHEAD)]
    for g in range(DEPTH * SLOTS + 1):
        plan += evac.get(g, []) + fin.get(g, [])
        if g + AHEAD < DEPTH * SLOTS:
            plan.append(("split", *divmod(g + AHEAD, SLOTS)))
        if g < DEPTH * SLOTS:
            plan += pre.get(g, []) + [("chunk", *divmod(g, SLOTS))]
        plan += sorted(pe.get(g, []), key=lambda x: first_used.get(x[0], 2))
    return plan


PLAN = make_plan()


def build(nc, xt, w_stream, params, lam_rows, consts, out):
    F32, F32R = mybir.dt.float32, mybir.dt.float32r
    ALU, ACT, AX = mybir.AluOpType, mybir.ActivationFunctionType, mybir.AxisListType

    ctx = ExitStack()

    def sb(name, shape, dt=F32):
        return ctx.enter_context(nc.sbuf_tensor(name, shape, dt))

    def bank(name):
        return ctx.enter_context(nc.psum_tensor(name, [128, 512], F32))

    def sem(name):
        return ctx.enter_context(nc.semaphore(name))

    raw = sb("raw", [128, RAW, 2 * CHUNK])
    w_hi = sb("w_hi", [128, RING, CHUNK], F32R)
    w_lo = sb("w_lo", [128, RING, CHUNK], F32R)
    x = sb("x", [128, KT, L])
    h_hi = sb("h_hi", [128, KT, L], F32R)
    h_lo = sb("h_lo", [128, KT, L], F32R)
    y_hi = sb("y_hi", [128, KT, L], F32R)
    y_lo = sb("y_lo", [128, KT, L], F32R)
    con = sb("con", [128, N_CONST])
    par = sb("par", [128, DEPTH * N_PAR])
    q_st = sb("q_st", [128, 4, L])
    k_st = sb("k_st", [128, 4, L])
    v_st = sb("v_st", [128, 3, 4 * 128])
    g_st = sb("g_st", [128, 4, L])
    c_st = sb("c_st", [128, 8, L])
    row = sb("row", [128, 2, L + 16])
    sq = sb("sq", [128, 3, L])
    qw = sb("qw", [128, L])
    rn = sb("rn", [128, L])
    ta = sb("ta", [128, L + 16])
    tb = sb("tb", [128, L + 16])
    gate_e = sb("gate_e", [128, L])
    pooled = sb("pooled", [128, L])
    probs = sb("probs", [128, 2, 2, L])
    p_t = sb("p_t", [128, 2, 3 * 128])
    acc = sb("acc", [128, L])
    rinv = sb("rinv", [128, L])
    d_w = sb("d_w", [128, DEPTH, 4 * 128])
    stat = sb("stat", [128, 8])
    lam_in = p_t[:, :, :].rearrange("p a b -> p (a b)")[:, 0:DEPTH * 256]
    lam_sum = sb("lam_sum", [128, DEPTH * 2])
    neg_lam = sb("neg_lam", [128, DEPTH])
    sub_w = sb("sub_w", [128, DEPTH])
    eps_c = sb("eps_c", [128, 1])

    dense = [bank("dense0"), bank("dense1")]
    norm_ps, swap_ps = bank("norm_ps"), bank("swap_ps")
    s_ps = [bank("s_ps0"), bank("s_ps1")]
    t_ps, o_ps = bank("t_ps"), bank("o_ps")

    def const(name, n=L):
        return con[:, CC[name]:CC[name] + n]

    ident, ones, halves = const("ident", 128), const("ones", 128), const("halves", 128)
    swap = {"a": const("swap8", 128), "b": const("swap32", 128), "c": const("swap32", 128)}

    def pcol(l, name, i=0):
        c = l * N_PAR + PC[name] + i
        return par[:, c:c + 1]

    LATENT = {"cq": (0, 3), "ckv": (3, 2)}
    SCALE = {"a": 64 ** -0.5, "b": 128 ** -0.5, "c": 192 ** -0.5}

    def pair_view(t, n):
        return t[:, 0:256].rearrange("p (m q) -> p m q", m=2)[:, :, 0:n]

    s_const, s_par, s_lam, s_dw = sem("s_const"), sem("s_par"), sem("s_lam"), sem("s_dw")
    s_x = [sem(f"s_x{i}") for i in range(4)]
    s_raw = [sem(f"s_raw{i}") for i in range(RAW)]
    s_stored = sem("s_stored")
    hi_ready, lo_ready, chunk_done = sem("hi_ready"), sem("lo_ready"), sem("chunk_done")
    tile_done = sem("tile_done")
    evac_done = sem("evac_done")
    up_taken = sem("up_taken")
    xt_taken = sem("xt_taken")
    sq_x = sem("sq_x")
    h_hi_ready, h_ready = sem("h_hi_ready"), sem("h_ready")
    acc_ready, xsum_done, rinv_ready = sem("acc_ready"), sem("xsum_done"), sem("rinv_ready")
    pre_done, stat_done, rn_ready, fin_done = sem("pre_done"), sem("stat_done"), sem("rn_ready"), sem("fin_done")
    turned_v, v_ready = sem("turned_v"), sem("v_ready")
    gate_exp, gate_done = sem("gate_exp"), sem("gate_done")
    pooled_ready, mixed_ps, mixed = sem("pooled_ready"), sem("mixed_ps"), sem("mixed")
    scores_ready, bias_ready, exp_done, w_ready = (sem("scores_ready"), sem("bias_ready"),
                                                   sem("exp_done"), sem("w_ready"))
    turned_p, pt_ready, pv_done, o_taken = sem("turned_p"), sem("pt_ready"), sem("pv_done"), sem("o_taken")
    y_hi_done, y_ready = sem("y_hi_done"), sem("y_ready")
    act_own, dve_own = sem("act_own"), sem("dve_own")
    lam_ready, lam_exp = sem("lam_ready"), sem("lam_exp")

    UP_TILES = 13

    def up_tiles(c):
        return [2, 2, 2, 4, 3][c]

    def up_no(c, j):
        return sum(up_tiles(i) for i in range(c)) + j + 1

    def chunk_size(s):
        kind, a, _ = chunk_kind(s)
        return 768 if kind == "up" and a < 3 else CHUNK

    def chunk_kind(s):
        u0 = pair_slot(3) + 4
        if u0 <= s < u0 + U_CHUNKS:
            return "up", s - u0, 0
        if s >= pair_slot(N_PAIRS):
            return ("out", *divmod(s - pair_slot(N_PAIRS), 4))
        return ("in", *divmod(s - (U_CHUNKS if s > u0 else 0), 4))

    u_end = pair_slot(3) + 4 + U_CHUNKS

    def entry(l, s):
        n = s + (1 if s >= u_end else 0)
        return l * ENTRIES + n // 2, n % 2

    evacs_of = {"in": 0, "up": 0, "out": 0}
    bank_of, freed_by, tile_no = {}, {}, {}
    n_tile = 0
    for l in range(DEPTH):
        for s in range(SLOTS):
            kind, a, b = chunk_kind(s)
            if kind == "up":
                members = [(kind, a, j) for j in range(up_tiles(a))]
            elif b == 3:
                members = [(kind, a, j) for j in (0, 1)]
            else:
                members = []
            for m in members:
                evacs_of[m[0]] += 1
                tile_no[(l, *m)] = n_tile
                freed_by[n_tile] = (m[0], evacs_of[m[0]])
                n_tile += 1
    taken = {"in": evac_done, "up": up_taken, "out": xt_taken}

    steps = [(l, n, *st) for l in range(DEPTH) for n, st in enumerate(score_steps(l))]
    step_no = {(l, n): i for i, (l, n, *_) in enumerate(steps)}

    def last_step_using(l, branch, store, i):
        best = 0
        for k, (ll, n, s, b, h, qi) in enumerate(steps):
            if ll != l or b != branch:
                continue
            if b == "a":
                used = {h}
            elif b == "b" and store in ("k", "v"):
                used = {h // 2}
            else:
                used = {h, h + 1}
            if i in used:
                best = k + 1
        return best

    before = {"a": "c", "b": "a", "c": "b"}

    def store_free(l, branch, store, i):
        prev = before[branch]
        if prev == "b":
            return last_step_using(l - 1, prev, store, i) if l else 0
        return last_step_using(l, prev, store, i)

    norm_order, swap_order, pre_no, fin_no, gate_no = {}, {}, {}, {}, {}
    stats_before, fins_before, evac_no, v_no = {}, {}, {}, {}
    for stg in PLAN:
        stats_before[stg], fins_before[stg] = len(norm_order), len(fin_no)
        if stg[0] in ("rope_stat", "lat_stat", "sub_stat", "xsum"):
            norm_order[stg] = len(norm_order)
        if stg[0] in ("v_turn", "mix") or (stg[0] == "rope_stat" and stg[2] not in ("qn", "kn")):
            swap_order[stg] = len(swap_order)
        if stg[0] in ("rope_pre", "lat_pre", "sub_pre"):
            pre_no[stg[:4] if stg[0] == "rope_pre" else stg] = len(pre_no) + 1
        if stg[0] in ("rope_fin", "lat_fin", "sub_fin"):
            fin_no[stg] = len(fin_no) + 1
        if stg[0] == "gate":
            gate_no[stg] = len(gate_no) + 1
        if stg[0] == "evac":
            evac_no[stg[1:]] = len(evac_no) + 1
        if stg[0] == "v_out":
            v_no[stg[1:]] = len(v_no) + 1
    n_evac = {(l, *PAIRS[p], j): n for (l, p, j), n in evac_no.items()}
    swap_list = list(swap_order)
    takes_swap = {"rope_stat": fin_done, "v_turn": v_ready, "mix": mixed}

    def swap_taken_value(stage):
        if stage[0] == "rope_stat":
            return fin_no[("rope_fin", *stage[1:])]
        if stage[0] == "v_turn":
            return v_no[stage[1:4]]
        return 4 * stage[1] + stage[2] + 1

    def evac_of(l, kind, i):
        if kind == "kr":
            return n_evac[(l, "cqr", 2, 1)]
        return next(n for (ll, k, i0, j), n in n_evac.items() if ll == l and k == kind and i0 + j == i)

    rope = {"aq": ("a", 64), "ak": ("a", 64), "bq": ("b", 128), "bk": ("b", 128), "kr": ("c", 64),
            "qr": ("c", 64), "qn": (None, 128), "kn": (None, 128)}

    def rope_source(key, i, j):
        if j is not None:
            return row[:, j, 8:8 + L]
        return rope_target(key, i)

    def rope_target(key, i):
        if key in ("aq", "bq", "qn"):
            return q_st[:, i, :]
        if key in ("ak", "bk", "kn"):
            return k_st[:, i, :]
        return c_st[:, 5, :] if key == "kr" else c_st[:, 6 + i, :]

    def rope_from(l, key):
        return first_query(l) if key in ("aq", "bq", "qn", "qr") else 0

    def gate_from(l):
        return first_query(l)

    def tile_from(l, kind):
        return first_query(l) if kind in ("aq", "bq", "ag", "bg", "cg", "dg") else 0

    def uses_row(kind):
        return kind not in ("cq", "ckv", "cqr")

    def previous_row(l, p):
        while True:
            p -= 1
            if p < 0:
                l, p = l - 1, N_PAIRS - 1
            if l < 0:
                return None
            if uses_row(PAIRS[p][0]):
                return l, p

    o_before, n_o = [], 0
    for k, (l, n, _, b, h, i) in enumerate(steps):
        o_before.append(n_o)
        n_o += 1 if b != "a" or i == len(query_tiles(l)) - 1 else 0

    def needs_of(branch, h):
        return {"a": [("aq", h), ("ak", h)],
                "b": [("bq", h), ("bq", h + 1), ("bk", h // 2)],
                "c": [("qn", h), ("qn", h + 1), ("kn", h), ("kn", h + 1), ("qr", h // 2), ("kr", 0)]}[branch]

    def rows_of(kind, i):
        return {"a": 0, "b": 4, "c": 8, "d": 12}[kind] + i

    y_count, n_y = {}, 0
    for stg in PLAN:
        l = stg[1]
        if stg[0] == "lat_fin":
            n_y += 1
            y_count[(l, stg[2])] = n_y
        elif stg[0] in ("head_out", "sub_fin"):
            n_y += 1
            y_count[(l, "acb".index(score_steps(l)[stg[2]][1]))] = n_y
            y_count[stg] = n_y
        elif stg[0] == "gate" and stg[2] == "dg":
            n_y += 1
            y_count[(l, 3, stg[3])] = n_y
            y_count[stg] = n_y
    branch_of_chunk = {0: 0, 1: 2, 2: 1}

    tile_sem, n_mid, g = {}, 0, 0
    for l in range(DEPTH):
        for s in range(SLOTS):
            g += 1
            kind, a, b = chunk_kind(s)
            n = up_tiles(a) if kind == "up" else (2 if b == 3 else 0)
            for j in range(n):
                if j < n - 1:
                    n_mid += 1
                    tile_sem[(l, kind, a, j)] = (tile_done, n_mid)
                else:
                    tile_sem[(l, kind, a, j)] = (chunk_done, g)

    def wait_tile(eng, l, kind, a, j):
        which, n = tile_sem[(l, kind, a, j)]
        eng.wait_ge(which, n)
        return dense[tile_no[(l, kind, a, j)] % 2]

    block = ctx.enter_context(nc.Block())

    @block.sync
    def _(sp):
        sp.dma_start(x[:, 0:4, :], xt[:, 0:4, :]).then_inc(s_x[0], 16)
        sp.dma_start(par[:, :], params).then_inc(s_par, 16)
        for e in range(DEPTH * ENTRIES):
            if e >= RAW:
                l, n = divmod(e - RAW, ENTRIES)
                s_last = 2 * n + 1 - (1 if 2 * n + 1 >= u_end else 0)
                if 2 * n + 1 == u_end:
                    s_last = u_end - 1
                sp.wait_ge(lo_ready, l * SLOTS + s_last + 1)
            sp.dma_start(raw[:, e % RAW, :], w_stream[e, :, :]).then_inc(s_raw[e % RAW], 16)
            if e < 3:
                sp.dma_start(x[:, 4 * e + 4:4 * e + 8, :], xt[:, 4 * e + 4:4 * e + 8, :]).then_inc(s_x[e + 1], 16)
            if e == 2:
                sp.dma_start(con[:, :], consts[:, 0:N_CONST]).then_inc(s_const, 16)
                sp.dma_start(lam_in, lam_rows).then_inc(s_lam, 16)
                sp.dma_start(d_w[:, :, :], consts[:, N_CONST:].rearrange("p (l c) -> p l c", l=DEPTH)).then_inc(s_dw, 16)
        q0 = first_query(DEPTH - 1)
        for n in range(O_PAIRS):
            sp.wait_ge(xt_taken, 2 * O_PAIRS * (DEPTH - 1) + 2 * n + 2)
            sp.dma_start(out[:, 2 * n:2 * n + 2, :], x[:, 2 * n:2 * n + 2, q0:L]).then_inc(s_stored, 16)
        sp.wait_ge(s_stored, 16 * O_PAIRS)

    @block.tensor
    def _(pe):
        def three(ps, whi, wlo, xhi, xlo, first, last):
            nc.tensor.matmul(ps, whi, xhi, start=first, stop=False)
            nc.tensor.matmul(ps, whi, xlo, start=False, stop=False)
            return nc.tensor.matmul(ps, wlo, xhi, start=False, stop=last)

        def bank_for(tile):
            if tile >= 2:
                kind, n = freed_by[tile - 2]
                pe.wait_ge(taken[kind], n)
            return dense[tile % 2]

        def chunk(l, s):
            kind, a, b = chunk_kind(s)
            g = l * SLOTS + s
            pe.wait_ge(lo_ready, g + 1)
            hi, lo = w_hi[:, g % RING, :], w_lo[:, g % RING, :]
            if kind == "up":
                mm = up_chunk(l, a, hi, lo)
            else:
                xhi, xlo = (h_hi, h_lo) if kind == "in" else (y_hi, y_lo)
                t0 = tile_from(l, PAIRS[a][0]) if kind == "in" else first_query(l)
                for j in (0, 1):
                    tile = tile_no[(l, kind, a, j)]
                    ps = bank_for(tile) if b == 0 else dense[tile % 2]
                    for k in range(CK):
                        kt = CK * b + k
                        if a == 0 and j == 0 and kind == "in":
                            pe.wait_ge(h_ready, KT * l + kt + 1)
                        if a == 0 and j == 0 and kind == "out":
                            if b < 3 and k == 0:
                                pe.wait_ge(y_ready, y_count[(l, branch_of_chunk[b])])
                            elif b == 3:
                                pe.wait_ge(y_ready, y_count[(l, 3, k)])
                        c = 256 * k + 128 * j
                        mm = three(ps[:, 0:L - t0], hi[:, c:c + 128], lo[:, c:c + 128],
                                   xhi[:, kt, t0:L], xlo[:, kt, t0:L], kt == 0, kt == KT - 1)
                    if b == 3 and j == 0:
                        mm.then_inc(tile_done, 1)
            mm.then_inc(chunk_done, 1)

        def up_chunk(l, c, hi, lo):
            if c == 0:
                pe.wait_ge(y_ready, y_count[(l, "cq")])
            if c == 3:
                pe.wait_ge(y_ready, y_count[(l, "ckv")])
            q0 = first_query(l)
            for j in range(up_tiles(c)):
                ps = bank_for(tile_no[(l, "up", c, j)])
                if c < 3:
                    for k in range(3):
                        w = slice(256 * k + 128 * j, 256 * k + 128 * j + 128)
                        mm = three(ps[:, 0:L - q0], hi[:, w], lo[:, w],
                                   y_hi[:, k, q0:L], y_lo[:, k, q0:L], k == 0, k == 2)
                elif c == 3:
                    for k in range(2):
                        w = slice(512 * k + 128 * j, 512 * k + 128 * j + 128)
                        mm = three(ps[:, 0:L], hi[:, w], lo[:, w],
                                   y_hi[:, 3 + k, :], y_lo[:, 3 + k, :], k == 0, k == 1)
                else:
                    t, n = K_BLOCKS[j]
                    for k in range(2):
                        w = slice(512 * k, 512 * k + 512)
                        mm = three(ps[0:n, :], y_hi[:, 3 + k, t:t + n], y_lo[:, 3 + k, t:t + n],
                                   hi[:, w], lo[:, w], k == 0, k == 1)
                if j < up_tiles(c) - 1:
                    mm.then_inc(tile_done, 1)
            return mm

        def norm_free(*stage):
            n = norm_order[stage]
            if n:
                pe.wait_ge(rn_ready, n)

        def swap_free(*stage):
            n = swap_order[stage]
            if n:
                prev = swap_list[n - 1]
                pe.wait_ge(takes_swap[prev[0]], swap_taken_value(prev))

        def xsum(l):
            pe.wait_ge(acc_ready, KT * (l + 1))
            norm_free("xsum", l)
            nc.tensor.matmul(norm_ps[:, 0:L], ones, acc[:, :], start=True, stop=True).then_inc(stat_done, 1)

        def rope_stat(l, key, i):
            branch, width = rope[key]
            t0 = rope_from(l, key)
            pe.wait_ge(pre_done, pre_no[("rope_pre", l, key, i)])
            norm_free("rope_stat", l, key, i)
            sums = nc.tensor.matmul(norm_ps[:, t0:L], halves if width == 64 else ones, sq[:, 0, t0:L],
                                    start=True, stop=True)
            if branch:
                swap_free("rope_stat", l, key, i)
                sums = nc.tensor.matmul(swap_ps[:, t0:L], swap[branch], qw[:, t0:L], start=True, stop=True)
            sums.then_inc(stat_done, 1)

        def lat_stat(l, key):
            pe.wait_ge(pre_done, pre_no[("lat_pre", l, key)])
            norm_free("lat_stat", l, key)
            n = 3 if key == "cq" else 2
            for k in range(n):
                mm = nc.tensor.matmul(norm_ps[:, 0:L], ones, sq[:, k, :], start=k == 0, stop=k == n - 1)
            mm.then_inc(stat_done, 1)

        def v_turn(l, kind, i, j):
            pe.wait_ge(evac_done, evac_of(l, kind, i))
            swap_free("v_turn", l, kind, i, j)
            for b, (t, n) in enumerate(K_BLOCKS):
                mm = nc.tensor.transpose(swap_ps[0:n, 128 * b:128 * b + 128], row[:, j, 8 + t:8 + t + n], ident)
            mm.then_inc(turned_v, 1)

        def mix(l, g):
            pe.wait_ge(pooled_ready, 4 * l + g + 1)
            if l == 0 and g == 0:
                pe.wait_ge(s_dw, 16)
            swap_free("mix", l, g)
            nc.tensor.matmul(swap_ps[:, 0:L], d_w[:, l, 128 * g:128 * g + 128], pooled[:, :],
                             start=True, stop=True).then_inc(mixed_ps, 1)

        def score(l, n):
            _, branch, h, i = score_steps(l)[n]
            q, nq = query_tiles(l)[i]
            k = step_no[(l, n)]
            for key, hh in needs_of(branch, h):
                pe.wait_ge(fin_done, fin_no[("rope_fin", l, key, hh)])
            if k:
                pe.wait_ge(exp_done, 2 * k)
                if steps[k - 1][3] != "a":
                    pe.wait_ge(pt_ready, k)
            for m in (0, 1):
                ps = s_ps[m][0:nq, 0:L]
                if branch == "a":
                    half = slice(64 * m, 64 * m + 64)
                    mm = nc.tensor.matmul(ps, q_st[half, h, q:q + nq], k_st[half, h, :], start=True, stop=True)
                elif branch == "b":
                    mm = nc.tensor.matmul(ps, q_st[:, h + m, q:q + nq], k_st[:, h // 2, :], start=True, stop=True)
                else:
                    half = slice(64 * m, 64 * m + 64)
                    nc.tensor.matmul(ps, q_st[:, h + m, q:q + nq], k_st[:, h + m, :], start=True, stop=False)
                    mm = nc.tensor.matmul(ps, c_st[half, 6 + h // 2, q:q + nq], c_st[half, 5, :],
                                          start=False, stop=True)
            mm.then_inc(scores_ready, 1)

        def p_turn(l, n):
            _, branch, h, i = score_steps(l)[n]
            q, nq = query_tiles(l)[i]
            k = step_no[(l, n)]
            pe.wait_ge(w_ready, k + 1)
            if k:
                pe.wait_ge(pt_ready, k)
            for m in range(1 if branch == "a" else 2):
                ps = (t_ps, s_ps[1])[m]
                for b, (t, nk) in enumerate(K_BLOCKS):
                    mm = nc.tensor.transpose(ps[0:nk, 128 * b:128 * b + nq],
                                             probs[0:nq, k % 2, m, t:t + nk], ident[0:nq, 0:nq])
            mm.then_inc(turned_p, 1)

        def pv(l, n):
            _, branch, h, i = score_steps(l)[n]
            q, nq = query_tiles(l)[i]
            k = step_no[(l, n)]
            pe.wait_ge(pt_ready, k + 1)
            if branch == "c":
                pe.wait_ge(up_taken, UP_TILES * (l + 1))
            else:
                pe.wait_ge(v_ready, v_no[(l, "av", h) if branch == "a" else (l, "bv", h // 2)])
            if o_before[k]:
                pe.wait_ge(o_taken, o_before[k])
            for m in range(1 if branch == "a" else 2):
                vh = h // 2 if branch == "b" else h + m
                c = q if branch == "a" else 128 * m
                for b, (t, nk) in enumerate(K_BLOCKS):
                    mm = nc.tensor.matmul(o_ps[:, c:c + nq], v_st[0:nk, b, 128 * vh:128 * vh + 128],
                                          p_t[0:nk, m, 128 * b:128 * b + nq], start=b == 0, stop=b == 2)
            mm.then_inc(pv_done, 1)

        def sub_stat(l, n):
            pe.wait_ge(pre_done, pre_no[("sub_pre", l, n)])
            norm_free("sub_stat", l, n)
            t0 = first_query(l)
            nc.tensor.matmul(norm_ps[:, t0:L], ones, sq[:, 0, t0:L], start=True, stop=True).then_inc(stat_done, 1)

        pe.wait_ge(s_const, 16)
        run = dict(chunk=chunk, xsum=xsum, rope_stat=rope_stat, lat_stat=lat_stat, v_turn=v_turn, mix=mix,
                   score=score, p_turn=p_turn, pv=pv, sub_stat=sub_stat)
        for stage, *what in PLAN:
            if stage in run:
                run[stage](*what)

    @block.scalar
    def _(act):
        own = [0]

        def link(ins):
            own[0] += 1
            ins.then_inc(act_own, 1)
            act.wait_ge(act_own, own[0])

        def signal(ins, which, n):
            ins.then_inc(which, 1)
            act.wait_ge(which, n)

        def setup(_):
            nc.scalar.preload_act_table_set("natural_log_exp_and_others")
            act.wait_ge(s_par, 16)
            for kt in range(KT):
                act.wait_ge(s_x[kt // 4], 16)
                x_tile(0, kt)
            act.wait_ge(lam_ready, 1)
            signal(nc.scalar.activation(lam_sum[:, :], lam_sum[:, :], ACT.Exp), lam_exp, 1)

        def x_tile(l, kt):
            n = KT * l + kt
            if n > 1:
                act.wait_ge(acc_ready, n - 1)
            signal(nc.scalar.activation(sq[:, kt % 2, :], x[:, kt, :], ACT.Square), sq_x, n + 1)
            signal(nc.scalar.activation(h_hi[:, kt, :], x[:, kt, :], ACT.Copy, scale=pcol(l, "norm", kt)),
                   h_hi_ready, n + 1)

        def x_out(l, n):
            if l < DEPTH - 1:
                for kt in (2 * n, 2 * n + 1):
                    act.wait_ge(xt_taken, KT * l + kt + 1)
                    x_tile(l + 1, kt)

        def split(l, s):
            g = l * SLOTS + s
            e, half = entry(l, s)
            n = chunk_size(s)
            act.wait_ge(s_raw[e % RAW], 16 * (e // RAW + 1))
            if g >= RING:
                act.wait_ge(chunk_done, g - RING + 1)
            signal(nc.scalar.activation(w_hi[:, g % RING, 0:n], raw[:, e % RAW, CHUNK * half:CHUNK * half + n],
                                        ACT.Copy), hi_ready, g + 1)

        def up_out(l, c):
            for j in range(up_tiles(c)):
                ps = wait_tile(act, l, "up", c, j)
                q0 = first_query(l)
                if c < 2:
                    i, out_ = 2 * c + j, q_st[:, 2 * c + j, q0:L]
                    free = (scores_ready, store_free(l, "c", "q", i))
                elif c == 2:
                    out_, free = c_st[:, 6 + j, q0:L], (scores_ready, store_free(l, "c", "q", j))
                elif c == 3:
                    out_, free = k_st[:, j, :], (scores_ready, store_free(l, "c", "k", j))
                else:
                    n = K_BLOCKS[j][1]
                    out_, free = v_st[0:n, j, :], (pv_done, store_free(l, "c", "v", 3))
                if free[1]:
                    act.wait_ge(*free)
                src = ps[0:K_BLOCKS[j][1], :] if c == 4 else ps[:, 0:L - q0] if c < 3 else ps[:, 0:L]
                signal(nc.scalar.activation(out_, src, ACT.Copy), up_taken, UP_TILES * l + up_no(c, j))

        def buffers_free(*stage):
            if stats_before[stage]:
                act.wait_ge(stat_done, stats_before[stage])
            if fins_before[stage]:
                act.wait_ge(fin_done, fins_before[stage])

        def rope_pre(l, key, i, j):
            branch, width = rope[key]
            t0 = rope_from(l, key)
            if key in ("qn", "kn", "qr"):
                pass
            else:
                act.wait_ge(evac_done, evac_of(l, key, i))
            buffers_free("rope_pre", l, key, i, j)
            src = rope_source(key, i, j)[:, t0:L]
            square = nc.scalar.activation(sq[:, 0, t0:L], src, ACT.Square)
            if branch:
                link(square)
                square = nc.scalar.activation(qw[:, t0:L], src, ACT.Copy, scale=pcol(l, key if key != "kr" else "kr"))
            signal(square, pre_done, pre_no[("rope_pre", l, key, i)])

        def lat_pre(l, key):
            k0, n = LATENT[key]
            act.wait_ge(evac_done, evac_no[(l, 2, 0) if key == "cq" else (l, 1, 1)])
            buffers_free("lat_pre", l, key)
            signal(nc.scalar.activation(sq[:, 0:n, :], c_st[:, k0:k0 + n, :], ACT.Square), pre_done,
                   pre_no[("lat_pre", l, key)])

        def sub_pre(l, n):
            t0 = first_query(l)
            act.wait_ge(pv_done, step_no[(l, n)] + 1)
            buffers_free("sub_pre", l, n)
            signal(nc.scalar.activation(sq[:, 0, t0:L], o_ps[:, t0:L], ACT.Square), pre_done,
                   pre_no[("sub_pre", l, n)])

        def inverse_root(stat_stage, fin_stage, width, t0, out_):
            n = norm_order[stat_stage]
            act.wait_ge(stat_done, n + 1)
            if fins_before[fin_stage]:
                act.wait_ge(fin_done, fins_before[fin_stage])
            link(nc.scalar.activation(rn[:, t0:L], norm_ps[:, t0:L], ACT.Ln, scale=1.0 / width, bias=eps_c[:, 0:1]))
            signal(nc.scalar.activation(out_, rn[:, t0:L], ACT.Exp, scale=-0.5), rn_ready, n + 1)

        def xscale(l):
            if l:
                act.wait_ge(evac_done, 2 * N_PAIRS * l)
            inverse_root(("xsum", l), ("xscale", l), D_MODEL, 0, rinv[:, :])

        def rope_fin(l, key, i):
            t0 = rope_from(l, key)
            inverse_root(("rope_stat", l, key, i), ("rope_fin", l, key, i), rope[key][1], t0, rn[:, t0:L])

        def lat_fin(l, key):
            k0, n = LATENT[key]
            inverse_root(("lat_stat", l, key), ("lat_fin", l, key), 128 * n, 0, rn[:, :])
            if l:
                act.wait_ge(chunk_done, SLOTS * l)
            act.wait_ge(fin_done, fin_no[("lat_fin", l, key)])
            y_high(y_hi[:, k0:k0 + n, :], c_st[:, k0:k0 + n, :], y_count[(l, key)])

        def y_high(out_, src, n):
            signal(nc.scalar.activation(out_, src, ACT.Copy), y_hi_done, n)

        def sub_fin(l, n):
            h = score_steps(l)[n][2]
            t0 = first_query(l)
            inverse_root(("sub_stat", l, n), ("sub_fin", l, n), 128, t0, rn[:, t0:L])
            act.wait_ge(fin_done, fin_no[("sub_fin", l, n)])
            act.wait_ge(chunk_done, SLOTS * l + u_end)
            y_high(y_hi[:, rows_of("a", h), t0:L], tb[:, t0:L], y_count[("sub_fin", l, n)])

        def head_out(l, n):
            _, b, h, i = score_steps(l)[n]
            q, nq = query_tiles(l)[i]
            r = rows_of(b, h)
            act.wait_ge(o_taken, o_before[step_no[(l, n)]] + 1)
            act.wait_ge(chunk_done, SLOTS * l + u_end)
            y_high(y_hi[:, r:r + 2, q:q + nq], pair_view(ta, nq), y_count[("head_out", l, n)])

        def gate(l, kind, i, j):
            t0 = gate_from(l)
            n = gate_no[("gate", l, kind, i, j)]
            act.wait_ge(evac_done, evac_of(l, kind, i))
            if n > 1:
                act.wait_ge(gate_done, n - 1)
            signal(nc.scalar.activation(gate_e[:, t0:L], row[:, j, 8 + t0:8 + L], ACT.Exp, scale=-1.0), gate_exp, n)
            if kind == "dg":
                act.wait_ge(gate_done, n)
                act.wait_ge(chunk_done, SLOTS * l + u_end)
                y_high(y_hi[:, rows_of("d", i), t0:L], ta[:, t0:L], y_count[("gate", l, kind, i, j)])

        def v_out(l, kind, i):
            act.wait_ge(turned_v, v_no[(l, kind, i)])
            free = store_free(l, kind[0], "v", i)
            if free:
                act.wait_ge(pv_done, free)
            c = slice(128 * i, 128 * i + 128)
            link(nc.scalar.activation(v_st[:, 0:2, c], swap_ps[:, 0:256].rearrange("p (b d) -> p b d", b=2), ACT.Copy))
            signal(nc.scalar.activation(v_st[0:16, 2, c], swap_ps[0:16, 256:384], ACT.Copy), v_ready,
                   v_no[(l, kind, i)])

        def mix_out(l, g):
            n = 4 * l + g + 1
            act.wait_ge(mixed_ps, n)
            act.wait_ge(y_ready, y_count[(l, "ckv")])
            signal(nc.scalar.activation(c_st[:, g, :], swap_ps[:, 0:L], ACT.Copy, scale=pcol(l, "dsc", g)), mixed, n)

        def softmax(l, n):
            k = step_no[(l, n)]
            _, b, h, i = score_steps(l)[n]
            nq = query_tiles(l)[i][1]
            act.wait_ge(bias_ready, k + 1)
            if k >= 2:
                act.wait_ge(turned_p, k - 1)
            for m in (0, 1):
                signal(nc.scalar.activation(probs[0:nq, k % 2, m, :], s_ps[m][0:nq, 0:L], ACT.Exp,
                                            bias=stat[0:nq, 2 + m:3 + m], scale=SCALE[b],
                                            accum_out=stat[0:nq, 4 + m:5 + m]), exp_done, 2 * k + m + 1)

        def p_out(l, n):
            k = step_no[(l, n)]
            _, b, h, i = score_steps(l)[n]
            nq = query_tiles(l)[i][1]
            act.wait_ge(turned_p, k + 1)
            if k:
                act.wait_ge(pv_done, k)
            for m in range(1 if b == "a" else 2):
                ps = (t_ps, s_ps[1])[m]
                link(nc.scalar.activation(p_t[:, m, 0:256].rearrange("p (b q) -> p b q", b=2)[:, :, 0:nq],
                                          ps[:, 0:256].rearrange("p (b q) -> p b q", b=2)[:, :, 0:nq], ACT.Copy))
                tail = nc.scalar.activation(p_t[0:16, m, 256:256 + nq], ps[0:16, 256:256 + nq], ACT.Copy)
                if m == 0 and b != "a":
                    link(tail)
            signal(tail, pt_ready, k + 1)

        run = dict(setup=setup, x_out=x_out, split=split, up_out=up_out, rope_pre=rope_pre, lat_pre=lat_pre,
                   sub_pre=sub_pre, xscale=xscale, rope_fin=rope_fin, lat_fin=lat_fin, sub_fin=sub_fin,
                   head_out=head_out, gate=gate, v_out=v_out, mix_out=mix_out, softmax=softmax, p_out=p_out)
        for stage, *what in PLAN:
            if stage in run:
                run[stage](*what)

    @block.vector
    def _(dve):
        own = [0]

        def link(ins):
            own[0] += 1
            ins.then_inc(dve_own, 1)
            dve.wait_ge(dve_own, own[0])

        def signal(ins, which, n):
            ins.then_inc(which, 1)
            dve.wait_ge(which, n)

        def setup(_):
            link(nc.vector.memset(eps_c[:, :], EPS))
            link(nc.vector.memset(row[:, :, :], 0.0))
            dve.wait_ge(s_par, 16)
            for kt in range(KT):
                x_tile(0, kt)
            dve.wait_ge(s_lam, 16)
            for l in range(DEPTH):
                v = lam_in.rearrange("p (l a b d) -> p l a b d", l=DEPTH, a=2, b=2)
                for a in (0, 1):
                    link(nc.vector.tensor_tensor(ta[:, 0:64], v[:, l, a, 0, :], v[:, l, a, 1, :], ALU.mult))
                    link(nc.vector.reduce_sum(lam_sum[:, 2 * l + a:2 * l + a + 1], ta[:, 0:64], AX.X))
            signal(nc.vector.memset(stat[:, :], 0.0), lam_ready, 1)
            dve.wait_ge(lam_exp, 1)
            for l in range(DEPTH):
                li = lambda_init(l)
                c = slice(l, l + 1)
                link(nc.vector.tensor_tensor(neg_lam[:, c], lam_sum[:, 2 * l + 1:2 * l + 2],
                                             lam_sum[:, 2 * l:2 * l + 1], ALU.subtract))
                link(nc.vector.tensor_scalar(neg_lam[:, c], neg_lam[:, c], -li, None, ALU.add))
                link(nc.vector.tensor_scalar(sub_w[:, c], pcol(l, "sub"), 1.0 - li, None, ALU.mult))

        def x_tile(l, kt):
            n = KT * l + kt
            dve.wait_ge(sq_x, n + 1)
            if kt == 0:
                if l:
                    dve.wait_ge(stat_done, norm_order[("xsum", l - 1)] + 1)
                add = nc.vector.tensor_copy(acc[:, :], sq[:, 0, :])
            else:
                add = nc.vector.tensor_tensor(acc[:, :], acc[:, :], sq[:, kt % 2, :], ALU.add)
            signal(add, acc_ready, n + 1)
            dve.wait_ge(h_hi_ready, n + 1)
            signal(nc.vector.scalar_tensor_tensor(h_lo[:, kt, :], x[:, kt, :], pcol(l, "norm", kt),
                                                  h_hi[:, kt, :].bitcast(F32), ALU.mult, ALU.subtract),
                   h_ready, n + 1)

        def x_out(l, n):
            t0 = first_query(l)
            for j in (0, 1):
                kt = 2 * n + j
                ps = wait_tile(dve, l, "out", n, j)
                signal(nc.vector.tensor_tensor(x[:, kt, t0:L], x[:, kt, t0:L], ps[:, 0:L - t0], ALU.add),
                       xt_taken, KT * l + kt + 1)
            if l < DEPTH - 1:
                for kt in (2 * n, 2 * n + 1):
                    x_tile(l + 1, kt)

        def split(l, s):
            g = l * SLOTS + s
            e, half = entry(l, s)
            n = chunk_size(s)
            dve.wait_ge(hi_ready, g + 1)
            signal(nc.vector.tensor_tensor(w_lo[:, g % RING, 0:n], raw[:, e % RAW, CHUNK * half:CHUNK * half + n],
                                           w_hi[:, g % RING, 0:n].bitcast(F32), ALU.subtract), lo_ready, g + 1)

        def evac(l, p, j):
            kind, i0 = PAIRS[p]
            ps = wait_tile(dve, l, "in", p, j)
            t0 = tile_from(l, kind)
            dve.wait_ge(rn_ready, norm_order[("xsum", l)] + 1)
            if kind in ("cq", "ckv", "cqr"):
                c = {"cq": j, "ckv": 3 + j, "cqr": (2, 5)[j]}[kind]
                if c == 5 and l:
                    dve.wait_ge(scores_ready, last_step_using(l - 1, "c", "k", 3))
                out_ = c_st[:, c, t0:L]
            else:
                prev = previous_row(l, p)
                if prev:
                    pk, pi = PAIRS[prev[1]]
                    i = pi + j
                    if pk in ("aq", "ak", "bq", "bk"):
                        dve.wait_ge(pre_done, pre_no[("rope_pre", prev[0], pk, i)])
                    elif pk in ("av", "bv"):
                        dve.wait_ge(turned_v, v_no[(prev[0], pk, i)])
                out_ = row[:, j, 8 + t0:8 + L]
            signal(nc.vector.tensor_tensor(out_, ps[:, 0:L - t0], rinv[:, t0:L], ALU.mult), evac_done,
                   evac_no[(l, p, j)])

        def rope_fin(l, key, i):
            branch, width = rope[key]
            t0 = rope_from(l, key)
            out_ = rope_target(key, i)[:, t0:L]
            store = {"q": "q", "k": "k"}[key[-1] if key in ("aq", "ak", "bq", "bk") else "q"]
            dve.wait_ge(rn_ready, norm_order[("rope_stat", l, key, i)] + 1)
            if branch:
                cos, sin = const("cos_" + branch)[:, t0:L], const("sin_" + branch)[:, t0:L]
                link(nc.vector.tensor_tensor(ta[:, t0:L], swap_ps[:, t0:L], sin, ALU.mult))
                link(nc.vector.tensor_tensor(tb[:, t0:L], qw[:, t0:L], cos, ALU.mult))
                link(nc.vector.tensor_tensor(tb[:, t0:L], tb[:, t0:L], ta[:, t0:L], ALU.add))
                if branch in "ab":
                    free = store_free(l, branch, store, i)
                    if free:
                        dve.wait_ge(scores_ready, free)
                last = nc.vector.tensor_tensor(out_, tb[:, t0:L], rn[:, t0:L], ALU.mult)
            else:
                last = nc.vector.scalar_tensor_tensor(out_, out_, pcol(l, key), rn[:, t0:L], ALU.mult, ALU.mult)
            signal(last, fin_done, fin_no[("rope_fin", l, key, i)])

        def y_low(out_, src, hi_, n):
            dve.wait_ge(y_hi_done, n)
            signal(nc.vector.tensor_tensor(out_, src, hi_, ALU.subtract), y_ready, n)

        def lat_fin(l, key):
            k0, n = LATENT[key]
            dve.wait_ge(rn_ready, norm_order[("lat_stat", l, key)] + 1)
            for k in range(k0, k0 + n):
                ins = nc.vector.scalar_tensor_tensor(c_st[:, k, :], c_st[:, k, :], pcol(l, key, k - k0), rn[:, :],
                                                     ALU.mult, ALU.mult)
                if k < k0 + n - 1:
                    link(ins)
            signal(ins, fin_done, fin_no[("lat_fin", l, key)])
            y_low(y_lo[:, k0:k0 + n, :], c_st[:, k0:k0 + n, :], y_hi[:, k0:k0 + n, :].bitcast(F32), y_count[(l, key)])

        def sub_fin(l, n):
            h = score_steps(l)[n][2]
            t0 = first_query(l)
            dve.wait_ge(rn_ready, norm_order[("sub_stat", l, n)] + 1)
            signal(nc.vector.scalar_tensor_tensor(ta[:, t0:L], o_ps[:, t0:L], sub_w[:, l:l + 1], rn[:, t0:L],
                                                  ALU.mult, ALU.mult), o_taken, o_before[step_no[(l, n)]] + 1)
            signal(nc.vector.tensor_tensor(tb[:, t0:L], ta[:, t0:L], g_st[:, h, t0:L], ALU.mult), fin_done,
                   fin_no[("sub_fin", l, n)])
            r = rows_of("a", h)
            y_low(y_lo[:, r, t0:L], tb[:, t0:L], y_hi[:, r, t0:L].bitcast(F32), y_count[("sub_fin", l, n)])

        def head_out(l, n):
            _, b, h, i = score_steps(l)[n]
            q, nq = query_tiles(l)[i]
            r = rows_of(b, h)
            k = step_no[(l, n)]
            dve.wait_ge(pv_done, k + 1)
            signal(nc.vector.tensor_tensor(pair_view(ta, nq), pair_view(o_ps, nq), g_st[:, h:h + 2, q:q + nq],
                                           ALU.mult), o_taken, o_before[k] + 1)
            y_low(y_lo[:, r:r + 2, q:q + nq], pair_view(ta, nq), y_hi[:, r:r + 2, q:q + nq].bitcast(F32),
                  y_count[("head_out", l, n)])

        def gate(l, kind, i, j):
            t0 = gate_from(l)
            n = gate_no[("gate", l, kind, i, j)]
            g = row[:, j, 8 + t0:8 + L]
            e = gate_e[:, t0:L]
            dve.wait_ge(gate_exp, n)
            link(nc.vector.tensor_scalar(e, e, 1.0, None, ALU.add))
            link(nc.vector.reciprocal(e, e))
            if kind != "dg":
                signal(nc.vector.tensor_tensor(g_st[:, i, t0:L], g, e, ALU.mult), gate_done, n)
                return
            link(nc.vector.tensor_tensor(ta[:, t0:L], g, e, ALU.mult))
            dve.wait_ge(mixed, 4 * l + i + 1)
            signal(nc.vector.tensor_tensor(ta[:, t0:L], ta[:, t0:L], c_st[:, i, t0:L], ALU.mult), gate_done, n)
            r = rows_of("d", i)
            y_low(y_lo[:, r, t0:L], ta[:, t0:L], y_hi[:, r, t0:L].bitcast(F32), y_count[("gate", l, kind, i, j)])

        def pool(l, g, j):
            u = row[:, j, :]
            wide = L + 16
            link(nc.vector.tensor_tensor(ta[:, 1:wide], u[:, 0:wide - 1], u[:, 1:wide], ALU.add))
            src, dst, lo, hi, step = ta, tb, 1, wide, 1
            for _ in range(g):
                link(nc.vector.tensor_tensor(dst[:, lo + step:hi - step], src[:, lo:hi - 2 * step],
                                             src[:, lo + 2 * step:hi], ALU.add))
                lo, hi, step = lo + step, hi - step, 2 * step
                src, dst = dst, src
            edge = con[:, CC["edge"] + 16 * g:CC["edge"] + 16 * g + 16]
            link(nc.vector.tensor_tensor(src[:, 8:16], src[:, 8:16], edge[:, 0:8], ALU.mult))
            link(nc.vector.tensor_tensor(src[:, L:L + 8], src[:, L:L + 8], edge[:, 8:16], ALU.mult))
            n = 4 * l + g
            if n:
                dve.wait_ge(mixed_ps, n)
            signal(nc.vector.scalar_tensor_tensor(pooled[:, :], src[:, 8:8 + L], 1.0 / (2 << g), u[:, 8:8 + L],
                                                  ALU.mult, ALU.subtract), pooled_ready, n + 1)

        def softmax(l, n):
            k = step_no[(l, n)]
            _, b, h, i = score_steps(l)[n]
            nq = query_tiles(l)[i][1]
            dve.wait_ge(scores_ready, k + 1)
            for m in (0, 1):
                link(nc.vector.reduce_max(stat[0:nq, m:m + 1], s_ps[m][0:nq, 0:L], AX.X))
            signal(nc.vector.tensor_scalar(stat[0:nq, 2:4], stat[0:nq, 0:2], -SCALE[b], None, ALU.mult),
                   bias_ready, k + 1)
            dve.wait_ge(exp_done, 2 * k + 2)
            link(nc.vector.reciprocal(stat[0:nq, 6:8], stat[0:nq, 4:6]))
            p = [probs[0:nq, k % 2, m, :] for m in (0, 1)]
            if b == "a":
                link(nc.vector.tensor_tensor(stat[0:nq, 7:8], stat[0:nq, 7:8], neg_lam[0:nq, l:l + 1], ALU.mult))
                link(nc.vector.tensor_scalar(p[1], p[1], stat[0:nq, 7:8], None, ALU.mult))
                last = nc.vector.scalar_tensor_tensor(p[0], p[0], stat[0:nq, 6:7], p[1], ALU.mult, ALU.add)
            else:
                link(nc.vector.tensor_scalar(p[0], p[0], stat[0:nq, 6:7], None, ALU.mult))
                last = nc.vector.tensor_scalar(p[1], p[1], stat[0:nq, 7:8], None, ALU.mult)
            signal(last, w_ready, k + 1)

        dve.wait_ge(s_x[0], 16)
        run = dict(setup=setup, x_out=x_out, split=split, evac=evac, rope_fin=rope_fin, lat_fin=lat_fin,
                   sub_fin=sub_fin, head_out=head_out, gate=gate, pool=pool, softmax=softmax)
        waited = [False]
        for stage, *what in PLAN:
            if stage == "rope_fin" and not waited[0]:
                dve.wait_ge(s_const, 16)
                waited[0] = True
            if stage in run:
                run[stage](*what)

    ctx.close()


def constants():
    def table(pos, dim, theta):
        inv = np.float32(theta) ** (-np.arange(0, dim, 2, dtype=np.float32) / np.float32(dim))
        ang = (pos.astype(np.float32)[:, None] * inv[None, :].astype(np.float32)).astype(np.float32)
        c, s = np.cos(ang.astype(np.float64)).T, np.sin(ang.astype(np.float64)).T
        return np.concatenate([c, c]), np.concatenate([-s, s])

    out = np.zeros((128, N_CONST), np.float32)

    def put(name, a):
        out[:, CC[name]:CC[name] + a.shape[1]] = a

    pos = np.arange(L)
    rot = 16
    c, s = table(pos, rot, 500000.0)
    cos_a, sin_a = np.ones((128, L)), np.zeros((128, L))
    for m in (0, 64):
        cos_a[m:m + rot], sin_a[m:m + rot] = c, s
    put("cos_a", cos_a)
    put("sin_a", sin_a)
    rows = np.concatenate([np.full(N_META, -1), np.repeat(np.arange(SEQ // GRID_W), GRID_W)])
    cols = np.concatenate([np.arange(N_META), np.tile(np.arange(GRID_W), SEQ // GRID_W)])
    (cr, sr), (cc, sc) = table(rows, 64, 10000.0), table(cols, 64, 10000.0)
    put("cos_b", np.concatenate([cr, cc]))
    put("sin_b", np.concatenate([sr, sc]))
    c, s = table(pos, 64, 500000.0)
    put("cos_c", np.concatenate([c, c]))
    put("sin_c", np.concatenate([s, s]))
    i = np.arange(128)
    put("ident", np.eye(128))
    put("ones", np.ones((128, 128)))
    put("halves", (i[:, None] // 64 == i[None, :] // 64).astype(np.float32))
    put("swap8", ((i[:, None] ^ 8) == i[None, :]).astype(np.float32))
    put("swap32", ((i[:, None] ^ 32) == i[None, :]).astype(np.float32))
    t = np.concatenate([np.arange(8), np.arange(L - 8, L)])
    for g in range(4):
        w = 2 << g
        n = np.clip(t + w - w // 2, 0, L) - np.clip(t - w // 2, 0, L)
        out[:, CC["edge"] + 16 * g:CC["edge"] + 16 * g + 16] = w / n.astype(np.float64)
    return out


def pack_weights(w_in, w_out, uq, ukv):
    stream = np.zeros((DEPTH * ENTRIES, 128, 2, CHUNK), w_in.dtype)
    for l in range(DEPTH):
        wi = w_in[l].reshape(KT, 128, -1)
        wo = w_out[l].reshape(KT, 128, -1)
        n = l * 2 * ENTRIES

        def add(block):
            nonlocal n
            b = block.transpose(1, 0, 2).reshape(128, -1)
            stream[n // 2, :, n % 2, :b.shape[1]] = b
            n += 1

        for p in range(N_PAIRS):
            kind, i = PAIRS[p]
            if kind == "cqr":
                a, r = OFF["cq"] + 256, OFF["ckr"]
                cols = np.concatenate([wi[:, :, a:a + 128], wi[:, :, r:r + 64], wi[:, :, r:r + 64]], axis=2)
            else:
                a = OFF[kind] + 128 * i
                cols = wi[:, :, a:a + 256]
            for b in range(KT // CK):
                add(cols[CK * b:CK * b + CK])
            if p == LEAD_PAIRS - 1:
                q = uq[l].reshape(3, 128, 4, 192)
                kv = ukv[l].reshape(2, 128, 4, 256)
                add(q[:, :, 0:2, 0:128].reshape(3, 128, 256))
                add(q[:, :, 2:4, 0:128].reshape(3, 128, 256))
                add(q[:, :, :, 128:].reshape(3, 128, 256))
                add(kv[:, :, :, 0:128].reshape(2, 128, 512))
                add(kv[:, :, :, 128:].reshape(2, 128, 512))
                n += 1
        for p in range(O_PAIRS):
            for b in range(KT // CK):
                add(wo[CK * b:CK * b + CK, :, 256 * p:256 * p + 256])
    return stream.reshape(DEPTH * ENTRIES, 128, 2 * CHUNK)


def pack_params(v):
    par = np.zeros((128, DEPTH, N_PAR), np.float32)

    def put(name, a):
        a = a.reshape(DEPTH, -1, 128).transpose(2, 0, 1)
        par[:, :, PC[name]:PC[name] + a.shape[2]] = a

    twice = lambda a: np.concatenate([a, a], axis=1)
    put("norm", v["norm_w"])
    put("aq", twice(v["a_q_norm"]))
    put("ak", twice(v["a_k_norm"]))
    put("sub", v["a_subln"])
    put("bq", v["b_q_norm"])
    put("bk", v["b_k_norm"])
    put("cq", v["c_q_lat_norm"])
    put("ckv", v["c_kv_lat_norm"])
    put("qn", v["c_q_norm"][:, :128])
    put("qr", twice(v["c_q_norm"][:, 128:]))
    put("kn", v["c_k_norm"][:, :128])
    put("kr", twice(v["c_k_norm"][:, 128:]))
    put("dsc", v["d_scale"])
    return par.reshape(128, DEPTH * N_PAR)


def kernel(**inputs):
    import concourse.bacc as _bacc
    from concourse.bass_utils import run_bass_kernel_spmd as _run

    v = {k: np.asarray(a) for k, a in inputs.items()}
    tokens = np.concatenate([v["meta_tokens"], v["x"][0]], axis=0)
    d_w = v["d_w_group"].transpose(2, 0, 1, 3).reshape(128, -1)
    arrays = {
        "xt": np.ascontiguousarray(tokens.reshape(L, KT, 128).transpose(2, 1, 0)),
        "w_stream": pack_weights(v["w_in"], v["w_out"], v["c_w_uq"], v["c_w_ukv"]),
        "params": pack_params(v),
        "lam_rows": np.ascontiguousarray(np.broadcast_to(v["a_lambda"].reshape(1, -1), (128, DEPTH * 256))),
        "consts": np.concatenate([constants(), d_w], axis=1),
    }
    nc = _bacc.Bacc("TRN2", target_bir_lowering=False, num_devices=1)
    args = [nc.dram_tensor(f"{n}_dram", a.shape, mybir.dt.from_np(a.dtype), kind="ExternalInput").ap()
            for n, a in arrays.items()]
    out = nc.dram_tensor("out_dram", (128, KT, SEQ), mybir.dt.float32, kind="ExternalOutput").ap()
    build(nc, *args, out)
    r = _run(nc, [{f"{n}_dram": a for n, a in arrays.items()}], core_ids=[0])
    got = r.results[0]["out_dram"]
    return np.ascontiguousarray(got.transpose(2, 1, 0)).reshape(1, SEQ, D_MODEL)
```

```python
import math
from contextlib import ExitStack

import concourse.bass as bass
import numpy as np
from concourse import mybir

D_MODEL, SEQ, DEPTH, N_META, GRID_W = 2048, 256, 2, 16, 64
L = N_META + SEQ
EPS = 1e-6
KT = D_MODEL // 128
CK = 4
CHUNK = CK * 256
N_PAIRS = 23
O_PAIRS = D_MODEL // 256
U_CHUNKS = 5
LEAD_PAIRS = 4
SLOTS = 4 * N_PAIRS + U_CHUNKS + 4 * O_PAIRS
ENTRIES = (SLOTS + 1) // 2
RAW, RING, AHEAD = 3, 4, 3
K_BLOCKS = [(0, 128), (128, 128), (256, L - 256)]

OFF = dict(aq=0, ak=512, av=1024, ag=1536, bq=2048, bk=2560, bv=2816, bg=3072, cq=3584, ckv=3968,
           ckr=4224, cg=4288, du=4800, dg=5312)
PAIRS = [("cq", 0), ("ckv", 0), ("cqr", 2), ("cg", 0), ("cg", 2), ("du", 0), ("du", 2),
         ("aq", 0), ("ak", 0), ("av", 0), ("ag", 0), ("aq", 2), ("ak", 2), ("av", 2), ("ag", 2),
         ("bk", 0), ("bv", 0), ("bq", 0), ("bg", 0), ("bq", 2), ("bg", 2), ("dg", 0), ("dg", 2)]

PC = dict(norm=0, aq=16, ak=17, sub=18, bq=19, bk=20, cq=21, ckv=24, qn=26, qr=27, kn=28, kr=29, dsc=30)
N_PAR = 34
CC = dict(cos_a=0, sin_a=L, cos_b=2 * L, sin_b=3 * L, cos_c=4 * L, sin_c=5 * L, ident=6 * L,
          ones=6 * L + 128, halves=6 * L + 256, swap8=6 * L + 384, swap32=6 * L + 512, edge=6 * L + 640)
N_CONST = 6 * L + 640 + 64


def lambda_init(layer):
    return 0.8 - 0.6 * math.exp(-0.3 * layer)


def pair_slot(p):
    return 4 * p + (U_CHUNKS if p >= LEAD_PAIRS else 0)


def first_query(layer):
    return N_META if layer == DEPTH - 1 else 0


def query_tiles(layer):
    q0 = first_query(layer)
    return [(q, min(128, L - q)) for q in range(q0, L, 128)]


def score_steps(layer):
    n = len(query_tiles(layer))
    first = {("c", 0): pair_slot(5) + 2, ("c", 2): pair_slot(7),
             ("a", 0): pair_slot(10) + 2, ("a", 1): pair_slot(12) + 2, ("a", 2): pair_slot(14) + 2,
             ("a", 3): pair_slot(16) + 2, ("b", 0): pair_slot(19), ("b", 2): pair_slot(21)}
    return [(s0 + 2 * i, b, h, i) for (b, h), s0 in first.items() for i in range(n)]


def make_plan():
    evac, fin, pre, pe = {}, {}, {}, {}

    def at(table, slot, stage):
        table.setdefault(slot, []).append(stage)

    for l in range(DEPTH):
        g0 = l * SLOTS
        at(pe, g0 + 2, ("xsum", l))
        at(fin, g0 + 3, ("xscale", l))
        for p, (kind, i0) in enumerate(PAIRS):
            end = g0 + pair_slot(p) + 3
            at(evac, end + 1, ("evac", l, p, 0))
            at(evac, end + 1, ("evac", l, p, 1))
            for j in (0, 1):
                s = end + 1 + j
                if kind in ("aq", "ak", "bq", "bk"):
                    at(pre, s, ("rope_pre", l, kind, i0 + j, j))
                    at(pe, s, ("rope_stat", l, kind, i0 + j))
                    at(fin, s + 1, ("rope_fin", l, kind, i0 + j))
                elif kind in ("av", "bv"):
                    at(pe, s, ("v_turn", l, kind, i0 + j, j))
                    at(fin, s + 1, ("v_out", l, kind, i0 + j))
                elif kind in ("ag", "bg", "cg", "dg"):
                    at(pre, s + j, ("gate", l, kind, i0 + j, j))
                    if kind == "dg":
                        at(pre, s + j, ("y_split", "gate", l, kind, i0 + j, j))
                elif kind == "du":
                    at(pre, s, ("pool", l, i0 + j, j))
                    at(pe, s + 1, ("mix", l, i0 + j))
                    at(fin, s + 2, ("mix_out", l, i0 + j))
        s = g0 + pair_slot(3)
        for n, key in enumerate(("cq", "ckv")):
            at(pre, s + n, ("lat_pre", l, key))
            at(pe, s + n, ("lat_stat", l, key))
            at(fin, s + n + 1, ("lat_fin", l, key))
            at(fin, s + n + 1, ("y_split", "lat_fin", l, key))
        at(pre, s + 2, ("rope_pre", l, "kr", 0, None))
        at(pe, s + 2, ("rope_stat", l, "kr", 0))
        at(fin, s + 3, ("rope_fin", l, "kr", 0))
        s = g0 + pair_slot(3) + 4
        for c in range(U_CHUNKS):
            at(evac, s + c + 1, ("up_out", l, c))
        posts = [("qn", 0), ("kn", 0), ("qr", 0), ("qn", 1), ("kn", 1),
                 ("qn", 2), ("kn", 2), ("qr", 1), ("qn", 3), ("kn", 3)]
        for n, (key, i) in enumerate(posts):
            s = g0 + pair_slot(4) + 1 + n
            at(pre, s, ("rope_pre", l, key, i, None))
            at(pe, s, ("rope_stat", l, key, i))
            at(fin, s + 1, ("rope_fin", l, key, i))
        last = len(query_tiles(l)) - 1
        for n, (s, b, h, i) in enumerate(score_steps(l)):
            s += g0
            at(pe, s, ("score", l, n))
            at(fin, s + 1, ("s_max", l, n))
            at(fin, s + 1, ("s_exp", l, n))
            at(fin, s + 1, ("s_scale", l, n))
            at(pe, s + 2, ("p_turn", l, n))
            at(fin, s + 3, ("p_out", l, n))
            at(pe, s + 3, ("pv", l, n))
            if b != "a":
                at(fin, s + 4, ("head_out", l, n))
                at(fin, s + 4, ("y_split", "head_out", l, n))
            elif i == last:
                s += 4
                while any(x[0] in ("rope_stat", "lat_stat", "sub_stat") for x in pe.get(s, [])):
                    s += 1
                at(pre, s, ("sub_pre", l, n))
                at(pe, s, ("sub_stat", l, n))
                at(fin, s + 1, ("sub_fin", l, n))
                at(fin, s + 1, ("y_split", "sub_fin", l, n))
        for n in range(O_PAIRS):
            at(evac, g0 + pair_slot(N_PAIRS) + 4 * n + 4, ("x_out", l, n))
    urgency = ["xscale", "evac", "up_out", "x_out", "s_max", "rope_fin", "lat_fin", "v_out", "mix_out", "sub_fin",
               "rope_pre", "lat_pre", "sub_pre", "p_out", "s_exp", "s_scale", "head_out", "pool", "y_split",
               "gate", "y_gate", "split"]
    pe_order = ["pv", "score", "p_turn"]
    slack = ("gate", "y_gate", "split")
    rank = lambda x: urgency.index("y_gate" if x[:2] == ("y_split", "gate") else x[0])
    plan = [("setup", 0)]
    for s in range(AHEAD + 1):
        plan += [("x_first", 0, s)] + [("split", 0, s)] * (s < AHEAD)
    for g in range(DEPTH * SLOTS + 1):
        now = fin.get(g, []) + pre.get(g, [])
        if g + AHEAD < DEPTH * SLOTS:
            now.append(("split", *divmod(g + AHEAD, SLOTS)))
        now.sort(key=rank)
        plan += [x for x in now if urgency[rank(x)] not in slack]
        if g < DEPTH * SLOTS:
            plan.append(("chunk", *divmod(g, SLOTS)))
        plan += evac.get(g + 1, [])
        plan += [x for x in now if urgency[rank(x)] in slack]
        plan += sorted(pe.get(g, []), key=lambda x: pe_order.index(x[0]) if x[0] in pe_order else -1)
    return plan


PLAN = make_plan()


def build(nc, xt, w_stream, params, lam_rows, consts, out):
    F32, F32R = mybir.dt.float32, mybir.dt.float32r
    ALU, ACT, AX = mybir.AluOpType, mybir.ActivationFunctionType, mybir.AxisListType

    ctx = ExitStack()

    def sb(name, shape, dt=F32):
        return ctx.enter_context(nc.sbuf_tensor(name, shape, dt))

    def bank(name):
        return ctx.enter_context(nc.psum_tensor(name, [128, 512], F32))

    def sem(name):
        return ctx.enter_context(nc.semaphore(name))

    raw = sb("raw", [128, RAW, 2 * CHUNK])
    w_hi = sb("w_hi", [128, RING, CHUNK], F32R)
    w_lo = sb("w_lo", [128, RING, CHUNK], F32R)
    x = sb("x", [128, KT, L])
    h_hi = sb("h_hi", [128, KT, L], F32R)
    h_lo = sb("h_lo", [128, KT, L], F32R)
    y_hi = sb("y_hi", [128, KT, L], F32R)
    y_lo = sb("y_lo", [128, KT, L], F32R)
    con = sb("con", [128, N_CONST])
    par = sb("par", [128, DEPTH * N_PAR])
    q_st = sb("q_st", [128, 4, L])
    k_st = sb("k_st", [128, 4, L])
    v_st = sb("v_st", [128, 3, 4 * 128])
    g_st = sb("g_st", [128, 4, L])
    c_st = sb("c_st", [128, 8, L])
    row = sb("row", [128, 2, L + 16])
    sq = sb("sq", [128, 3, L])
    qw = sb("qw", [128, 2, L])
    rn = sb("rn", [128, L])
    ta = sb("ta", [128, L + 16])
    tb = sb("tb", [128, L + 16])
    gate_e = sb("gate_e", [128, L])
    pooled = sb("pooled", [128, L])
    probs = sb("probs", [128, 2, 2, L])
    p_t = sb("p_t", [128, 2, 3 * 128])
    acc = sb("acc", [128, L])
    rinv = sb("rinv", [128, L])
    d_w = sb("d_w", [128, 4 * 128])
    yt = sb("yt", [128, L])
    stat = sb("stat", [128, 8])
    lam_in = p_t[:, :, :].rearrange("p a b -> p (a b)")[:, 0:DEPTH * 256]
    lam_sum = sb("lam_sum", [128, DEPTH * 2])
    neg_lam = sb("neg_lam", [128, DEPTH])
    sub_w = sb("sub_w", [128, DEPTH])
    eps_c = sb("eps_c", [128, 1])

    dense = [bank("dense0"), bank("dense1")]
    norm_ps, swap_ps = bank("norm_ps"), bank("swap_ps")
    s_ps = [bank("s_ps0"), bank("s_ps1")]
    t_ps, o_ps = bank("t_ps"), bank("o_ps")

    def const(name, n=L):
        return con[:, CC[name]:CC[name] + n]

    ident, ones, halves = const("ident", 128), const("ones", 128), const("halves", 128)
    swap = {"a": const("swap8", 128), "b": const("swap32", 128), "c": const("swap32", 128)}

    def pcol(l, name, i=0):
        c = l * N_PAR + PC[name] + i
        return par[:, c:c + 1]

    LATENT = {"cq": (0, 3), "ckv": (3, 2)}
    SCALE = {"a": 64 ** -0.5, "b": 128 ** -0.5, "c": 192 ** -0.5}

    def turned(m, b, nk, nq):
        if m == 0:
            return t_ps[0:nk, 128 * b:128 * b + nq]
        return o_ps[0:nk, 256 + 128 * b:256 + 128 * b + nq] if b < 2 else t_ps[0:nk, 384:384 + nq]

    def pair_view(t, n):
        return t[:, 0:256].rearrange("p (m q) -> p m q", m=2)[:, :, 0:n]

    s_const, s_par, s_lam, s_dw = sem("s_const"), sem("s_par"), sem("s_lam"), sem("s_dw")
    s_x = [sem(f"s_x{i}") for i in range(4)]
    s_raw = [sem(f"s_raw{i}") for i in range(RAW)]
    s_stored = sem("s_stored")
    hi_ready, lo_ready, chunk_done = sem("hi_ready"), sem("lo_ready"), sem("chunk_done")
    tile_done = sem("tile_done")
    evac_done = sem("evac_done")
    up_taken = sem("up_taken")
    xt_taken = sem("xt_taken")
    sq_x = sem("sq_x")
    h_hi_ready, h_ready = sem("h_hi_ready"), sem("h_ready")
    acc_ready, xsum_done, rinv_ready = sem("acc_ready"), sem("xsum_done"), sem("rinv_ready")
    pre_done, stat_done, rn_ready, fin_done = sem("pre_done"), sem("stat_done"), sem("rn_ready"), sem("fin_done")
    turned_v, v_ready = sem("turned_v"), sem("v_ready")
    gate_exp, gate_done = sem("gate_exp"), sem("gate_done")
    pooled_ready, mixed_ps, mixed = sem("pooled_ready"), sem("mixed_ps"), sem("mixed")
    scores_ready, bias_ready, exp_done, w_ready = (sem("scores_ready"), sem("bias_ready"),
                                                   sem("exp_done"), sem("w_ready"))
    turned_p, pt_ready, pv_done, o_taken = sem("turned_p"), sem("pt_ready"), sem("pv_done"), sem("o_taken")
    y_hi_done, y_ready = sem("y_hi_done"), sem("y_ready")
    act_own, dve_own = sem("act_own"), sem("dve_own")
    lam_ready, lam_exp = sem("lam_ready"), sem("lam_exp")

    UP_TILES = 13

    def up_tiles(c):
        return [2, 2, 2, 4, 3][c]

    def up_no(c, j):
        return sum(up_tiles(i) for i in range(c)) + j + 1

    def chunk_size(s):
        kind, a, _ = chunk_kind(s)
        return 768 if kind == "up" and a < 3 else CHUNK

    def chunk_kind(s):
        u0 = pair_slot(3) + 4
        if u0 <= s < u0 + U_CHUNKS:
            return "up", s - u0, 0
        if s >= pair_slot(N_PAIRS):
            return ("out", *divmod(s - pair_slot(N_PAIRS), 4))
        return ("in", *divmod(s - (U_CHUNKS if s > u0 else 0), 4))

    u_end = pair_slot(3) + 4 + U_CHUNKS

    def entry(l, s):
        n = s + (1 if s >= u_end else 0)
        return l * ENTRIES + n // 2, n % 2

    evacs_of = {"in": 0, "up": 0, "out": 0}
    bank_of, freed_by, tile_no = {}, {}, {}
    n_tile = 0
    for l in range(DEPTH):
        for s in range(SLOTS):
            kind, a, b = chunk_kind(s)
            if kind == "up":
                members = [(kind, a, j) for j in range(up_tiles(a))]
            elif b == 3:
                members = [(kind, a, j) for j in (0, 1)]
            else:
                members = []
            for m in members:
                evacs_of[m[0]] += 1
                tile_no[(l, *m)] = n_tile
                freed_by[n_tile] = (m[0], evacs_of[m[0]])
                n_tile += 1
    taken = {"in": evac_done, "up": up_taken, "out": xt_taken}

    steps = [(l, n, *st) for l in range(DEPTH) for n, st in enumerate(score_steps(l))]
    step_no = {(l, n): i for i, (l, n, *_) in enumerate(steps)}

    def last_step_using(l, branch, store, i):
        best = 0
        for k, (ll, n, s, b, h, qi) in enumerate(steps):
            if ll != l or b != branch:
                continue
            if b == "a":
                used = {h}
            elif b == "b" and store in ("k", "v"):
                used = {h // 2}
            else:
                used = {h, h + 1}
            if i in used:
                best = k + 1
        return best

    before = {"a": "c", "b": "a", "c": "b"}

    def store_free(l, branch, store, i):
        prev = before[branch]
        if prev == "b":
            return last_step_using(l - 1, prev, store, i) if l else 0
        return last_step_using(l, prev, store, i)

    norm_order, swap_order, pre_no, fin_no, gate_no = {}, {}, {}, {}, {}
    stats_before, fins_before, evac_no, v_no = {}, {}, {}, {}
    for stg in PLAN:
        stats_before[stg], fins_before[stg] = len(norm_order), len(fin_no)
        if stg[0] in ("rope_stat", "lat_stat", "sub_stat", "xsum"):
            norm_order[stg] = len(norm_order)
        if stg[0] in ("v_turn", "mix") or (stg[0] == "rope_stat" and stg[2] not in ("qn", "kn")):
            swap_order[stg] = len(swap_order)
        if stg[0] in ("rope_pre", "lat_pre", "sub_pre"):
            pre_no[stg[:4] if stg[0] == "rope_pre" else stg] = len(pre_no) + 1
        if stg[0] in ("rope_fin", "lat_fin", "sub_fin"):
            fin_no[stg] = len(fin_no) + 1
        if stg[0] == "gate":
            gate_no[stg] = len(gate_no) + 1
        if stg[0] == "evac":
            evac_no[stg[1:]] = len(evac_no) + 1
        if stg[0] == "v_out":
            v_no[stg[1:]] = len(v_no) + 1
    n_evac = {(l, *PAIRS[p], j): n for (l, p, j), n in evac_no.items()}
    norm_list = list(norm_order)

    def parity(*stage):
        return norm_order[stage] % 2

    def halves_free(*stage):
        n = norm_order[stage]
        lat = lambda k: k >= 0 and norm_list[k][0] == "lat_stat"
        stats = n if stage[0] == "lat_stat" or lat(n - 1) else n - 1
        fins = 0
        for m in range(n - 1):
            other = norm_list[m]
            if other[0] != "xsum":
                fins = max(fins, fin_no[(other[0].replace("stat", "fin"), *other[1:])])
        return stats, fins

    swap_list = list(swap_order)
    takes_swap = {"rope_stat": fin_done, "v_turn": v_ready, "mix": mixed}

    def swap_taken_value(stage):
        if stage[0] == "rope_stat":
            return fin_no[("rope_fin", *stage[1:])]
        if stage[0] == "v_turn":
            return v_no[stage[1:4]]
        return 4 * stage[1] + stage[2] + 1

    def evac_of(l, kind, i):
        if kind == "kr":
            return n_evac[(l, "cqr", 2, 1)]
        return next(n for (ll, k, i0, j), n in n_evac.items() if ll == l and k == kind and i0 + j == i)

    rope = {"aq": ("a", 64), "ak": ("a", 64), "bq": ("b", 128), "bk": ("b", 128), "kr": ("c", 64),
            "qr": ("c", 64), "qn": (None, 128), "kn": (None, 128)}

    def rope_source(key, i, j):
        if j is not None:
            return row[:, j, 8:8 + L]
        return rope_target(key, i)

    def rope_target(key, i):
        if key in ("aq", "bq", "qn"):
            return q_st[:, i, :]
        if key in ("ak", "bk", "kn"):
            return k_st[:, i, :]
        return c_st[:, 5, :] if key == "kr" else c_st[:, 6 + i, :]

    def rope_from(l, key):
        return first_query(l) if key in ("aq", "bq", "qn", "qr") else 0

    def gate_from(l):
        return first_query(l)

    def tile_from(l, kind):
        return first_query(l) if kind in ("aq", "bq", "ag", "bg", "cg", "dg") else 0

    def uses_row(kind):
        return kind not in ("cq", "ckv", "cqr")

    def previous_row(l, p):
        while True:
            p -= 1
            if p < 0:
                l, p = l - 1, N_PAIRS - 1
            if l < 0:
                return None
            if uses_row(PAIRS[p][0]):
                return l, p

    def y_tile(*source):
        n = y_count[source]
        if source[0] == "lat_fin":
            k0, m = LATENT[source[2]]
            return n, lambda y: y[:, k0:k0 + m, :], c_st[:, k0:k0 + m, :], (fin_done, fin_no[source])
        l = source[1]
        t0 = first_query(l)
        if source[0] == "gate":
            r = rows_of("d", source[3])
            return n, lambda y: y[:, r, t0:L], yt[:, t0:L], (gate_done, gate_no[source])
        _, b, h, i = score_steps(l)[source[2]]
        r = rows_of(b, h)
        if source[0] == "sub_fin":
            return n, lambda y: y[:, r, t0:L], yt[:, t0:L], (fin_done, fin_no[source])
        q, nq = query_tiles(l)[i]
        return (n, lambda y: y[:, r:r + 2, q:q + nq], pair_view(yt, nq),
                (o_taken, o_before[step_no[(l, source[2])]] + 1))

    o_before, n_o = [], 0
    for k, (l, n, _, b, h, i) in enumerate(steps):
        o_before.append(n_o)
        n_o += 1 if b != "a" or i == len(query_tiles(l)) - 1 else 0

    def needs_of(branch, h):
        return {"a": [("aq", h), ("ak", h)],
                "b": [("bq", h), ("bq", h + 1), ("bk", h // 2)],
                "c": [("qn", h), ("qn", h + 1), ("kn", h), ("kn", h + 1), ("qr", h // 2), ("kr", 0)]}[branch]

    def rows_of(kind, i):
        return {"a": 0, "b": 4, "c": 8, "d": 12}[kind] + i

    y_count, n_y = {}, 0
    for stg in PLAN:
        if stg[0] != "y_split":
            continue
        stg = stg[1:]
        l = stg[1]
        if stg[0] == "lat_fin":
            n_y += 1
            y_count[(l, stg[2])] = n_y
            y_count[stg] = n_y
        elif stg[0] in ("head_out", "sub_fin"):
            n_y += 1
            y_count[(l, "acb".index(score_steps(l)[stg[2]][1]))] = n_y
            y_count[stg] = n_y
        else:
            n_y += 1
            y_count[(l, 3, stg[3])] = n_y
            y_count[stg] = n_y
    branch_of_chunk = {0: 0, 1: 2, 2: 1}

    tile_sem, n_mid, g = {}, 0, 0
    for l in range(DEPTH):
        for s in range(SLOTS):
            g += 1
            kind, a, b = chunk_kind(s)
            n = up_tiles(a) if kind == "up" else (2 if b == 3 else 0)
            for j in range(n):
                if j < n - 1:
                    n_mid += 1
                    tile_sem[(l, kind, a, j)] = (tile_done, n_mid)
                else:
                    tile_sem[(l, kind, a, j)] = (chunk_done, g)

    def wait_tile(eng, l, kind, a, j):
        which, n = tile_sem[(l, kind, a, j)]
        eng.wait_ge(which, n)
        return dense[tile_no[(l, kind, a, j)] % 2]

    block = ctx.enter_context(nc.Block())

    @block.sync
    def _(sp):
        sp.dma_start(x[:, 0:4, :], xt[:, 0:4, :]).then_inc(s_x[0], 16)
        sp.dma_start(par[:, :], params).then_inc(s_par, 16)
        for e in range(DEPTH * ENTRIES):
            if e >= RAW:
                l, n = divmod(e - RAW, ENTRIES)
                s_last = 2 * n + 1 - (1 if 2 * n + 1 >= u_end else 0)
                if 2 * n + 1 == u_end:
                    s_last = u_end - 1
                sp.wait_ge(lo_ready, l * SLOTS + s_last + 1)
            if e % ENTRIES == 0 and e:
                l = e // ENTRIES
                sp.wait_ge(mixed_ps, 4 * l)
                sp.dma_start(d_w[:, :], consts[:, N_CONST + 512 * l:N_CONST + 512 * l + 512]).then_inc(s_dw, 16)
            sp.dma_start(raw[:, e % RAW, :], w_stream[e, :, :]).then_inc(s_raw[e % RAW], 16)
            if e < 3:
                sp.dma_start(x[:, 4 * e + 4:4 * e + 8, :], xt[:, 4 * e + 4:4 * e + 8, :]).then_inc(s_x[e + 1], 16)
            if e == 2:
                sp.dma_start(con[:, :], consts[:, 0:N_CONST]).then_inc(s_const, 16)
                sp.dma_start(lam_in, lam_rows).then_inc(s_lam, 16)
                sp.dma_start(d_w[:, :], consts[:, N_CONST:N_CONST + 512]).then_inc(s_dw, 16)
        q0 = first_query(DEPTH - 1)
        for n in range(O_PAIRS):
            sp.wait_ge(xt_taken, 2 * O_PAIRS * (DEPTH - 1) + 2 * n + 2)
            sp.dma_start(out[:, 2 * n:2 * n + 2, :], x[:, 2 * n:2 * n + 2, q0:L]).then_inc(s_stored, 16)
        sp.wait_ge(s_stored, 16 * O_PAIRS)

    @block.tensor
    def _(pe):
        def three(ps, whi, wlo, xhi, xlo, first, last):
            nc.tensor.matmul(ps, whi, xhi, start=first, stop=False)
            nc.tensor.matmul(ps, whi, xlo, start=False, stop=False)
            return nc.tensor.matmul(ps, wlo, xhi, start=False, stop=last)

        def bank_for(tile):
            if tile >= 2:
                kind, n = freed_by[tile - 2]
                pe.wait_ge(taken[kind], n)
            return dense[tile % 2]

        def chunk(l, s):
            kind, a, b = chunk_kind(s)
            g = l * SLOTS + s
            pe.wait_ge(lo_ready, g + 1)
            hi, lo = w_hi[:, g % RING, :], w_lo[:, g % RING, :]
            if kind == "up":
                mm = up_chunk(l, a, hi, lo)
            else:
                xhi, xlo = (h_hi, h_lo) if kind == "in" else (y_hi, y_lo)
                t0 = tile_from(l, PAIRS[a][0]) if kind == "in" else first_query(l)
                for j in (0, 1):
                    tile = tile_no[(l, kind, a, j)]
                    ps = bank_for(tile) if b == 0 else dense[tile % 2]
                    for k in range(CK):
                        kt = CK * b + k
                        if a == 0 and j == 0 and kind == "in":
                            pe.wait_ge(h_ready, KT * l + kt + 1)
                        if a == 0 and j == 0 and kind == "out":
                            if b < 3 and k == 0:
                                pe.wait_ge(y_ready, y_count[(l, branch_of_chunk[b])])
                            elif b == 3:
                                pe.wait_ge(y_ready, y_count[(l, 3, k)])
                        c = 256 * k + 128 * j
                        mm = three(ps[:, 0:L - t0], hi[:, c:c + 128], lo[:, c:c + 128],
                                   xhi[:, kt, t0:L], xlo[:, kt, t0:L], kt == 0, kt == KT - 1)
                    if b == 3 and j == 0:
                        mm.then_inc(tile_done, 1)
            mm.then_inc(chunk_done, 1)

        def up_chunk(l, c, hi, lo):
            if c == 0:
                pe.wait_ge(y_ready, y_count[(l, "cq")])
            if c == 3:
                pe.wait_ge(y_ready, y_count[(l, "ckv")])
            q0 = first_query(l)
            for j in range(up_tiles(c)):
                ps = bank_for(tile_no[(l, "up", c, j)])
                if c < 3:
                    for k in range(3):
                        w = slice(256 * k + 128 * j, 256 * k + 128 * j + 128)
                        mm = three(ps[:, 0:L - q0], hi[:, w], lo[:, w],
                                   y_hi[:, k, q0:L], y_lo[:, k, q0:L], k == 0, k == 2)
                elif c == 3:
                    for k in range(2):
                        w = slice(512 * k + 128 * j, 512 * k + 128 * j + 128)
                        mm = three(ps[:, 0:L], hi[:, w], lo[:, w],
                                   y_hi[:, 3 + k, :], y_lo[:, 3 + k, :], k == 0, k == 1)
                else:
                    t, n = K_BLOCKS[j]
                    for k in range(2):
                        w = slice(512 * k, 512 * k + 512)
                        mm = three(ps[0:n, :], y_hi[:, 3 + k, t:t + n], y_lo[:, 3 + k, t:t + n],
                                   hi[:, w], lo[:, w], k == 0, k == 1)
                if j < up_tiles(c) - 1:
                    mm.then_inc(tile_done, 1)
            return mm

        def norm_free(*stage):
            n = norm_order[stage]
            if n:
                pe.wait_ge(rn_ready, n)

        def swap_free(*stage):
            n = swap_order[stage]
            if n:
                prev = swap_list[n - 1]
                pe.wait_ge(takes_swap[prev[0]], swap_taken_value(prev))

        def xsum(l):
            pe.wait_ge(acc_ready, KT * (l + 1))
            pe.wait_ge(s_const, 16)
            norm_free("xsum", l)
            nc.tensor.matmul(norm_ps[:, 0:L], ones, acc[:, :], start=True, stop=True).then_inc(stat_done, 1)

        def rope_stat(l, key, i):
            branch, width = rope[key]
            t0 = rope_from(l, key)
            pe.wait_ge(pre_done, pre_no[("rope_pre", l, key, i)])
            norm_free("rope_stat", l, key, i)
            sums = nc.tensor.matmul(norm_ps[:, t0:L], halves if width == 64 else ones,
                                    sq[:, parity("rope_stat", l, key, i), t0:L],
                                    start=True, stop=True)
            if branch:
                swap_free("rope_stat", l, key, i)
                sums = nc.tensor.matmul(swap_ps[:, t0:L], swap[branch],
                                        qw[:, parity("rope_stat", l, key, i), t0:L], start=True, stop=True)
            sums.then_inc(stat_done, 1)

        def lat_stat(l, key):
            pe.wait_ge(pre_done, pre_no[("lat_pre", l, key)])
            norm_free("lat_stat", l, key)
            n = 3 if key == "cq" else 2
            for k in range(n):
                mm = nc.tensor.matmul(norm_ps[:, 0:L], ones, sq[:, k, :], start=k == 0, stop=k == n - 1)
            mm.then_inc(stat_done, 1)

        def v_turn(l, kind, i, j):
            pe.wait_ge(evac_done, evac_of(l, kind, i))
            swap_free("v_turn", l, kind, i, j)
            for b, (t, n) in enumerate(K_BLOCKS):
                mm = nc.tensor.transpose(swap_ps[0:n, 128 * b:128 * b + 128], row[:, j, 8 + t:8 + t + n], ident)
            mm.then_inc(turned_v, 1)

        def mix(l, g):
            pe.wait_ge(pooled_ready, 4 * l + g + 1)
            if g == 0:
                pe.wait_ge(s_dw, 16 * (l + 1))
            swap_free("mix", l, g)
            nc.tensor.matmul(swap_ps[:, 0:L], d_w[:, 128 * g:128 * g + 128], pooled[:, :],
                             start=True, stop=True).then_inc(mixed_ps, 1)

        def score(l, n):
            _, branch, h, i = score_steps(l)[n]
            q, nq = query_tiles(l)[i]
            k = step_no[(l, n)]
            for key, hh in needs_of(branch, h):
                pe.wait_ge(fin_done, fin_no[("rope_fin", l, key, hh)])
            if k:
                pe.wait_ge(exp_done, 2 * k)
            for m in (0, 1):
                ps = s_ps[m][0:nq, 0:L]
                if branch == "a":
                    half = slice(64 * m, 64 * m + 64)
                    mm = nc.tensor.matmul(ps, q_st[half, h, q:q + nq], k_st[half, h, :], start=True, stop=True)
                elif branch == "b":
                    mm = nc.tensor.matmul(ps, q_st[:, h + m, q:q + nq], k_st[:, h // 2, :], start=True, stop=True)
                else:
                    half = slice(64 * m, 64 * m + 64)
                    nc.tensor.matmul(ps, q_st[:, h + m, q:q + nq], k_st[:, h + m, :], start=True, stop=False)
                    mm = nc.tensor.matmul(ps, c_st[half, 6 + h // 2, q:q + nq], c_st[half, 5, :],
                                          start=False, stop=True)
            mm.then_inc(scores_ready, 1)

        def p_turn(l, n):
            _, branch, h, i = score_steps(l)[n]
            q, nq = query_tiles(l)[i]
            k = step_no[(l, n)]
            pe.wait_ge(w_ready, k + 1)
            if k:
                pe.wait_ge(pt_ready, k)
            for m in range(1 if branch == "a" else 2):
                if m and o_before[k]:
                    pe.wait_ge(o_taken, o_before[k])
                for b, (t, nk) in enumerate(K_BLOCKS):
                    mm = nc.tensor.transpose(turned(m, b, nk, nq),
                                             probs[0:nq, k % 2, m, t:t + nk], ident[0:nq, 0:nq])
            mm.then_inc(turned_p, 1)

        def pv(l, n):
            _, branch, h, i = score_steps(l)[n]
            q, nq = query_tiles(l)[i]
            k = step_no[(l, n)]
            pe.wait_ge(pt_ready, k + 1)
            if branch == "c":
                pe.wait_ge(up_taken, UP_TILES * (l + 1))
            else:
                pe.wait_ge(v_ready, v_no[(l, "av", h) if branch == "a" else (l, "bv", h // 2)])
            if o_before[k]:
                pe.wait_ge(o_taken, o_before[k])
            for m in range(1 if branch == "a" else 2):
                vh = h // 2 if branch == "b" else h + m
                c = q if branch == "a" else 128 * m
                for b, (t, nk) in enumerate(K_BLOCKS):
                    mm = nc.tensor.matmul(o_ps[:, c:c + nq], v_st[0:nk, b, 128 * vh:128 * vh + 128],
                                          p_t[0:nk, m, 128 * b:128 * b + nq], start=b == 0, stop=b == 2)
            mm.then_inc(pv_done, 1)

        def sub_stat(l, n):
            pe.wait_ge(pre_done, pre_no[("sub_pre", l, n)])
            norm_free("sub_stat", l, n)
            t0 = first_query(l)
            nc.tensor.matmul(norm_ps[:, t0:L], ones, sq[:, parity("sub_stat", l, n), t0:L], start=True, stop=True).then_inc(stat_done, 1)

        run = dict(chunk=chunk, xsum=xsum, rope_stat=rope_stat, lat_stat=lat_stat, v_turn=v_turn, mix=mix,
                   score=score, p_turn=p_turn, pv=pv, sub_stat=sub_stat)
        for stage, *what in PLAN:
            if stage in run:
                run[stage](*what)

    @block.scalar
    def _(act):
        own = [0]

        def link(ins):
            own[0] += 1
            ins.then_inc(act_own, 1)
            act.wait_ge(act_own, own[0])

        def signal(ins, which, n):
            ins.then_inc(which, 1)
            act.wait_ge(which, n)

        def setup(_):
            nc.scalar.preload_act_table_set("natural_log_exp_and_others")
            act.wait_ge(s_par, 16)

        def x_first(_, c):
            act.wait_ge(s_x[c], 16)
            for kt in range(4 * c, 4 * c + 4):
                x_tile(0, kt)
            if c == 3:
                act.wait_ge(lam_ready, 1)
                signal(nc.scalar.activation(lam_sum[:, :], lam_sum[:, :], ACT.Exp), lam_exp, 1)

        def x_tile(l, kt):
            n = KT * l + kt
            if n > 1:
                act.wait_ge(acc_ready, n - 1)
            signal(nc.scalar.activation(sq[:, kt % 2, :], x[:, kt, :], ACT.Square), sq_x, n + 1)
            signal(nc.scalar.activation(h_hi[:, kt, :], x[:, kt, :], ACT.Copy, scale=pcol(l, "norm", kt)),
                   h_hi_ready, n + 1)

        def x_out(l, n):
            if l < DEPTH - 1:
                for kt in (2 * n, 2 * n + 1):
                    act.wait_ge(xt_taken, KT * l + kt + 1)
                    x_tile(l + 1, kt)

        def split(l, s):
            g = l * SLOTS + s
            e, half = entry(l, s)
            n = chunk_size(s)
            act.wait_ge(s_raw[e % RAW], 16 * (e // RAW + 1))
            if g >= RING:
                act.wait_ge(chunk_done, g - RING + 1)
            signal(nc.scalar.activation(w_hi[:, g % RING, 0:n], raw[:, e % RAW, CHUNK * half:CHUNK * half + n],
                                        ACT.Copy), hi_ready, g + 1)

        def up_out(l, c):
            for j in range(up_tiles(c)):
                ps = wait_tile(act, l, "up", c, j)
                q0 = first_query(l)
                if c < 2:
                    i, out_ = 2 * c + j, q_st[:, 2 * c + j, q0:L]
                    free = (scores_ready, store_free(l, "c", "q", i))
                elif c == 2:
                    out_, free = c_st[:, 6 + j, q0:L], (scores_ready, store_free(l, "c", "q", j))
                elif c == 3:
                    out_, free = k_st[:, j, :], (scores_ready, store_free(l, "c", "k", j))
                else:
                    n = K_BLOCKS[j][1]
                    out_, free = v_st[0:n, j, :], (pv_done, store_free(l, "c", "v", 3))
                if free[1]:
                    act.wait_ge(*free)
                src = ps[0:K_BLOCKS[j][1], :] if c == 4 else ps[:, 0:L - q0] if c < 3 else ps[:, 0:L]
                signal(nc.scalar.activation(out_, src, ACT.Copy), up_taken, UP_TILES * l + up_no(c, j))

        def buffers_free(*stage):
            stats, fins = halves_free(*stage)
            if stats > 0:
                act.wait_ge(stat_done, stats)
            if fins:
                act.wait_ge(fin_done, fins)

        def rope_pre(l, key, i, j):
            branch, width = rope[key]
            t0 = rope_from(l, key)
            if key in ("qn", "kn", "qr"):
                pass
            else:
                act.wait_ge(evac_done, evac_of(l, key, i))
            buffers_free("rope_stat", l, key, i)
            half = parity("rope_stat", l, key, i)
            src = rope_source(key, i, j)[:, t0:L]
            square = nc.scalar.activation(sq[:, half, t0:L], src, ACT.Square)
            if branch:
                link(square)
                square = nc.scalar.activation(qw[:, half, t0:L], src, ACT.Copy, scale=pcol(l, key))
            signal(square, pre_done, pre_no[("rope_pre", l, key, i)])

        def lat_pre(l, key):
            k0, n = LATENT[key]
            act.wait_ge(evac_done, evac_no[(l, 2, 0) if key == "cq" else (l, 1, 1)])
            buffers_free("lat_stat", l, key)
            signal(nc.scalar.activation(sq[:, 0:n, :], c_st[:, k0:k0 + n, :], ACT.Square), pre_done,
                   pre_no[("lat_pre", l, key)])

        def sub_pre(l, n):
            t0 = first_query(l)
            act.wait_ge(pv_done, step_no[(l, n)] + 1)
            buffers_free("sub_stat", l, n)
            signal(nc.scalar.activation(sq[:, parity("sub_stat", l, n), t0:L], o_ps[:, t0:L], ACT.Square), pre_done,
                   pre_no[("sub_pre", l, n)])

        def inverse_root(stat_stage, fin_stage, width, t0, out_):
            n = norm_order[stat_stage]
            act.wait_ge(stat_done, n + 1)
            if fins_before[fin_stage]:
                act.wait_ge(fin_done, fins_before[fin_stage])
            link(nc.scalar.activation(rn[:, t0:L], norm_ps[:, t0:L], ACT.Ln, scale=1.0 / width, bias=eps_c[:, 0:1]))
            signal(nc.scalar.activation(out_, rn[:, t0:L], ACT.Exp, scale=-0.5), rn_ready, n + 1)

        def xscale(l):
            if l:
                act.wait_ge(evac_done, 2 * N_PAIRS * l)
            inverse_root(("xsum", l), ("xscale", l), D_MODEL, 0, rinv[:, :])

        def rope_fin(l, key, i):
            t0 = rope_from(l, key)
            inverse_root(("rope_stat", l, key, i), ("rope_fin", l, key, i), rope[key][1], t0, rn[:, t0:L])

        def lat_fin(l, key):
            k0, n = LATENT[key]
            inverse_root(("lat_stat", l, key), ("lat_fin", l, key), 128 * n, 0, rn[:, :])

        def sub_fin(l, n):
            t0 = first_query(l)
            inverse_root(("sub_stat", l, n), ("sub_fin", l, n), 128, t0, rn[:, t0:L])

        def y_split(*source):
            n, out_, src, ready = y_tile(*source)
            l = source[1]
            act.wait_ge(*ready)
            if source[0] != "lat_fin":
                act.wait_ge(chunk_done, SLOTS * l + u_end)
            elif l:
                act.wait_ge(chunk_done, SLOTS * l)
            signal(nc.scalar.activation(out_(y_hi), src, ACT.Copy), y_hi_done, n)

        def gate(l, kind, i, j):
            t0 = gate_from(l)
            n = gate_no[("gate", l, kind, i, j)]
            act.wait_ge(evac_done, evac_of(l, kind, i))
            if n > 1:
                act.wait_ge(gate_done, n - 1)
            signal(nc.scalar.activation(gate_e[:, t0:L], row[:, j, 8 + t0:8 + L], ACT.Exp, scale=-1.0), gate_exp, n)

        def v_out(l, kind, i):
            act.wait_ge(turned_v, v_no[(l, kind, i)])
            free = store_free(l, kind[0], "v", i)
            if free:
                act.wait_ge(pv_done, free)
            c = slice(128 * i, 128 * i + 128)
            link(nc.scalar.activation(v_st[:, 0:2, c], swap_ps[:, 0:256].rearrange("p (b d) -> p b d", b=2), ACT.Copy))
            signal(nc.scalar.activation(v_st[0:16, 2, c], swap_ps[0:16, 256:384], ACT.Copy), v_ready,
                   v_no[(l, kind, i)])

        def mix_out(l, g):
            n = 4 * l + g + 1
            act.wait_ge(mixed_ps, n)
            act.wait_ge(y_ready, y_count[(l, "ckv")])
            signal(nc.scalar.activation(c_st[:, g, :], swap_ps[:, 0:L], ACT.Copy, scale=pcol(l, "dsc", g)), mixed, n)

        def s_exp(l, n):
            k = step_no[(l, n)]
            _, b, h, i = score_steps(l)[n]
            nq = query_tiles(l)[i][1]
            act.wait_ge(bias_ready, k + 1)
            if k >= 2:
                act.wait_ge(turned_p, k - 1)
            for m in (0, 1):
                signal(nc.scalar.activation(probs[0:nq, k % 2, m, :], s_ps[m][0:nq, 0:L], ACT.Exp,
                                            bias=stat[0:nq, 2 + m:3 + m], scale=SCALE[b],
                                            accum_out=stat[0:nq, 4 + m:5 + m]), exp_done, 2 * k + m + 1)

        def p_out(l, n):
            k = step_no[(l, n)]
            _, b, h, i = score_steps(l)[n]
            nq = query_tiles(l)[i][1]
            act.wait_ge(turned_p, k + 1)
            if k:
                act.wait_ge(pv_done, k)
            for m in range(1 if b == "a" else 2):
                ps = (t_ps[:, 0:256], o_ps[:, 256:512])[m]
                link(nc.scalar.activation(p_t[:, m, 0:256].rearrange("p (b q) -> p b q", b=2)[:, :, 0:nq],
                                          ps.rearrange("p (b q) -> p b q", b=2)[:, :, 0:nq], ACT.Copy))
                tail = nc.scalar.activation(p_t[0:16, m, 256:256 + nq], turned(m, 2, 16, nq), ACT.Copy)
                if m == 0 and b != "a":
                    link(tail)
            signal(tail, pt_ready, k + 1)

        run = dict(setup=setup, x_first=x_first, x_out=x_out, split=split, up_out=up_out, rope_pre=rope_pre,
                   lat_pre=lat_pre, sub_pre=sub_pre, xscale=xscale, rope_fin=rope_fin, lat_fin=lat_fin,
                   sub_fin=sub_fin, y_split=y_split, gate=gate, v_out=v_out, mix_out=mix_out, s_exp=s_exp,
                   p_out=p_out)
        for stage, *what in PLAN:
            if stage in run:
                run[stage](*what)

    @block.vector
    def _(dve):
        own = [0]

        def link(ins):
            own[0] += 1
            ins.then_inc(dve_own, 1)
            dve.wait_ge(dve_own, own[0])

        def signal(ins, which, n):
            ins.then_inc(which, 1)
            dve.wait_ge(which, n)

        def setup(_):
            link(nc.vector.memset(eps_c[:, :], EPS))
            link(nc.vector.memset(row[:, :, :], 0.0))
            dve.wait_ge(s_par, 16)

        def x_first(_, c):
            dve.wait_ge(s_x[c], 16)
            for kt in range(4 * c, 4 * c + 4):
                x_tile(0, kt)
            if c == 3:
                lambdas()

        def lambdas():
            dve.wait_ge(s_lam, 16)
            for l in range(DEPTH):
                v = lam_in.rearrange("p (l a b d) -> p l a b d", l=DEPTH, a=2, b=2)
                for a in (0, 1):
                    link(nc.vector.tensor_tensor(ta[:, 0:64], v[:, l, a, 0, :], v[:, l, a, 1, :], ALU.mult))
                    link(nc.vector.reduce_sum(lam_sum[:, 2 * l + a:2 * l + a + 1], ta[:, 0:64], AX.X))
            signal(nc.vector.memset(stat[:, :], 0.0), lam_ready, 1)
            dve.wait_ge(lam_exp, 1)
            for l in range(DEPTH):
                li = lambda_init(l)
                c = slice(l, l + 1)
                link(nc.vector.tensor_tensor(neg_lam[:, c], lam_sum[:, 2 * l + 1:2 * l + 2],
                                             lam_sum[:, 2 * l:2 * l + 1], ALU.subtract))
                link(nc.vector.tensor_scalar(neg_lam[:, c], neg_lam[:, c], -li, None, ALU.add))
                link(nc.vector.tensor_scalar(sub_w[:, c], pcol(l, "sub"), 1.0 - li, None, ALU.mult))

        def x_tile(l, kt):
            n = KT * l + kt
            dve.wait_ge(sq_x, n + 1)
            if kt == 0:
                if l:
                    dve.wait_ge(stat_done, norm_order[("xsum", l - 1)] + 1)
                add = nc.vector.tensor_copy(acc[:, :], sq[:, 0, :])
            else:
                add = nc.vector.tensor_tensor(acc[:, :], acc[:, :], sq[:, kt % 2, :], ALU.add)
            signal(add, acc_ready, n + 1)
            dve.wait_ge(h_hi_ready, n + 1)
            signal(nc.vector.scalar_tensor_tensor(h_lo[:, kt, :], x[:, kt, :], pcol(l, "norm", kt),
                                                  h_hi[:, kt, :].bitcast(F32), ALU.mult, ALU.subtract),
                   h_ready, n + 1)

        def x_out(l, n):
            t0 = first_query(l)
            for j in (0, 1):
                kt = 2 * n + j
                ps = wait_tile(dve, l, "out", n, j)
                signal(nc.vector.tensor_tensor(x[:, kt, t0:L], x[:, kt, t0:L], ps[:, 0:L - t0], ALU.add),
                       xt_taken, KT * l + kt + 1)
            if l < DEPTH - 1:
                for kt in (2 * n, 2 * n + 1):
                    x_tile(l + 1, kt)

        def split(l, s):
            g = l * SLOTS + s
            e, half = entry(l, s)
            n = chunk_size(s)
            dve.wait_ge(hi_ready, g + 1)
            signal(nc.vector.tensor_tensor(w_lo[:, g % RING, 0:n], raw[:, e % RAW, CHUNK * half:CHUNK * half + n],
                                           w_hi[:, g % RING, 0:n].bitcast(F32), ALU.subtract), lo_ready, g + 1)

        def evac(l, p, j):
            kind, i0 = PAIRS[p]
            ps = wait_tile(dve, l, "in", p, j)
            t0 = tile_from(l, kind)
            dve.wait_ge(rn_ready, norm_order[("xsum", l)] + 1)
            if kind in ("cq", "ckv", "cqr"):
                c = {"cq": j, "ckv": 3 + j, "cqr": (2, 5)[j]}[kind]
                if c == 5 and l:
                    dve.wait_ge(scores_ready, last_step_using(l - 1, "c", "k", 3))
                out_ = c_st[:, c, t0:L]
            else:
                prev = previous_row(l, p)
                if prev:
                    pk, pi = PAIRS[prev[1]]
                    i = pi + j
                    if pk in ("aq", "ak", "bq", "bk"):
                        dve.wait_ge(pre_done, pre_no[("rope_pre", prev[0], pk, i)])
                    elif pk in ("av", "bv"):
                        dve.wait_ge(turned_v, v_no[(prev[0], pk, i)])
                out_ = row[:, j, 8 + t0:8 + L]
            signal(nc.vector.tensor_tensor(out_, ps[:, 0:L - t0], rinv[:, t0:L], ALU.mult), evac_done,
                   evac_no[(l, p, j)])

        def rope_fin(l, key, i):
            branch, width = rope[key]
            t0 = rope_from(l, key)
            out_ = rope_target(key, i)[:, t0:L]
            store = {"q": "q", "k": "k"}[key[-1] if key in ("aq", "ak", "bq", "bk") else "q"]
            if branch:
                half = parity("rope_stat", l, key, i)
                dve.wait_ge(stat_done, norm_order[("rope_stat", l, key, i)] + 1)
                cos, sin = const("cos_" + branch)[:, t0:L], const("sin_" + branch)[:, t0:L]
                link(nc.vector.tensor_tensor(ta[:, t0:L], swap_ps[:, t0:L], sin, ALU.mult))
                link(nc.vector.tensor_tensor(tb[:, t0:L], qw[:, half, t0:L], cos, ALU.mult))
                link(nc.vector.tensor_tensor(tb[:, t0:L], tb[:, t0:L], ta[:, t0:L], ALU.add))
                if branch in "ab":
                    free = store_free(l, branch, store, i)
                    if free:
                        dve.wait_ge(scores_ready, free)
            dve.wait_ge(rn_ready, norm_order[("rope_stat", l, key, i)] + 1)
            if branch:
                last = nc.vector.tensor_tensor(out_, tb[:, t0:L], rn[:, t0:L], ALU.mult)
            else:
                last = nc.vector.scalar_tensor_tensor(out_, out_, pcol(l, key), rn[:, t0:L], ALU.mult, ALU.mult)
            signal(last, fin_done, fin_no[("rope_fin", l, key, i)])

        def y_split(*source):
            n, out_, src, _ = y_tile(*source)
            dve.wait_ge(y_hi_done, n)
            signal(nc.vector.tensor_tensor(out_(y_lo), src, out_(y_hi).bitcast(F32), ALU.subtract), y_ready, n)

        def lat_fin(l, key):
            k0, n = LATENT[key]
            dve.wait_ge(rn_ready, norm_order[("lat_stat", l, key)] + 1)
            for k in range(k0, k0 + n):
                ins = nc.vector.scalar_tensor_tensor(c_st[:, k, :], c_st[:, k, :], pcol(l, key, k - k0), rn[:, :],
                                                     ALU.mult, ALU.mult)
                if k < k0 + n - 1:
                    link(ins)
            signal(ins, fin_done, fin_no[("lat_fin", l, key)])

        def sub_fin(l, n):
            h = score_steps(l)[n][2]
            t0 = first_query(l)
            dve.wait_ge(rn_ready, norm_order[("sub_stat", l, n)] + 1)
            signal(nc.vector.scalar_tensor_tensor(ta[:, t0:L], o_ps[:, t0:L], sub_w[:, l:l + 1], rn[:, t0:L],
                                                  ALU.mult, ALU.mult), o_taken, o_before[step_no[(l, n)]] + 1)
            signal(nc.vector.tensor_tensor(yt[:, t0:L], ta[:, t0:L], g_st[:, h, t0:L], ALU.mult), fin_done,
                   fin_no[("sub_fin", l, n)])

        def head_out(l, n):
            _, b, h, i = score_steps(l)[n]
            q, nq = query_tiles(l)[i]
            r = rows_of(b, h)
            k = step_no[(l, n)]
            dve.wait_ge(pv_done, k + 1)
            signal(nc.vector.tensor_tensor(pair_view(yt, nq), pair_view(o_ps, nq), g_st[:, h:h + 2, q:q + nq],
                                           ALU.mult), o_taken, o_before[k] + 1)

        def gate(l, kind, i, j):
            t0 = gate_from(l)
            n = gate_no[("gate", l, kind, i, j)]
            g = row[:, j, 8 + t0:8 + L]
            e = gate_e[:, t0:L]
            dve.wait_ge(gate_exp, n)
            link(nc.vector.tensor_scalar(e, e, 1.0, None, ALU.add))
            link(nc.vector.reciprocal(e, e))
            if kind != "dg":
                signal(nc.vector.tensor_tensor(g_st[:, i, t0:L], g, e, ALU.mult), gate_done, n)
                return
            link(nc.vector.tensor_tensor(ta[:, t0:L], g, e, ALU.mult))
            dve.wait_ge(mixed, 4 * l + i + 1)
            signal(nc.vector.tensor_tensor(yt[:, t0:L], ta[:, t0:L], c_st[:, i, t0:L], ALU.mult), gate_done, n)

        def pool(l, g, j):
            u = row[:, j, :]
            wide = L + 16
            link(nc.vector.tensor_tensor(ta[:, 1:wide], u[:, 0:wide - 1], u[:, 1:wide], ALU.add))
            src, dst, lo, hi, step = ta, tb, 1, wide, 1
            for _ in range(g):
                link(nc.vector.tensor_tensor(dst[:, lo + step:hi - step], src[:, lo:hi - 2 * step],
                                             src[:, lo + 2 * step:hi], ALU.add))
                lo, hi, step = lo + step, hi - step, 2 * step
                src, dst = dst, src
            edge = con[:, CC["edge"] + 16 * g:CC["edge"] + 16 * g + 16]
            link(nc.vector.tensor_tensor(src[:, 8:16], src[:, 8:16], edge[:, 0:8], ALU.mult))
            link(nc.vector.tensor_tensor(src[:, L:L + 8], src[:, L:L + 8], edge[:, 8:16], ALU.mult))
            n = 4 * l + g
            if n:
                dve.wait_ge(mixed_ps, n)
            signal(nc.vector.scalar_tensor_tensor(pooled[:, :], src[:, 8:8 + L], 1.0 / (2 << g), u[:, 8:8 + L],
                                                  ALU.mult, ALU.subtract), pooled_ready, n + 1)

        def s_max(l, n):
            k = step_no[(l, n)]
            _, b, h, i = score_steps(l)[n]
            nq = query_tiles(l)[i][1]
            dve.wait_ge(scores_ready, k + 1)
            for m in (0, 1):
                link(nc.vector.reduce_max(stat[0:nq, m:m + 1], s_ps[m][0:nq, 0:L], AX.X))
            signal(nc.vector.tensor_scalar(stat[0:nq, 2:4], stat[0:nq, 0:2], -SCALE[b], None, ALU.mult),
                   bias_ready, k + 1)

        def s_scale(l, n):
            k = step_no[(l, n)]
            _, b, h, i = score_steps(l)[n]
            nq = query_tiles(l)[i][1]
            dve.wait_ge(exp_done, 2 * k + 2)
            link(nc.vector.reciprocal(stat[0:nq, 6:8], stat[0:nq, 4:6]))
            p = [probs[0:nq, k % 2, m, :] for m in (0, 1)]
            if b == "a":
                link(nc.vector.tensor_tensor(stat[0:nq, 7:8], stat[0:nq, 7:8], neg_lam[0:nq, l:l + 1], ALU.mult))
                link(nc.vector.tensor_scalar(p[1], p[1], stat[0:nq, 7:8], None, ALU.mult))
                last = nc.vector.scalar_tensor_tensor(p[0], p[0], stat[0:nq, 6:7], p[1], ALU.mult, ALU.add)
            else:
                link(nc.vector.tensor_scalar(p[0], p[0], stat[0:nq, 6:7], None, ALU.mult))
                last = nc.vector.tensor_scalar(p[1], p[1], stat[0:nq, 7:8], None, ALU.mult)
            signal(last, w_ready, k + 1)

        dve.wait_ge(s_x[0], 16)
        run = dict(setup=setup, x_first=x_first, x_out=x_out, split=split, evac=evac, rope_fin=rope_fin,
                   lat_fin=lat_fin, sub_fin=sub_fin, head_out=head_out, y_split=y_split, gate=gate, pool=pool,
                   s_max=s_max, s_scale=s_scale)
        waited = [False]
        for stage, *what in PLAN:
            if stage == "rope_fin" and not waited[0]:
                dve.wait_ge(s_const, 16)
                waited[0] = True
            if stage in run:
                run[stage](*what)

    ctx.close()


def constants():
    def table(pos, dim, theta):
        inv = np.float32(theta) ** (-np.arange(0, dim, 2, dtype=np.float32) / np.float32(dim))
        ang = (pos.astype(np.float32)[:, None] * inv[None, :].astype(np.float32)).astype(np.float32)
        c, s = np.cos(ang.astype(np.float64)).T, np.sin(ang.astype(np.float64)).T
        return np.concatenate([c, c]), np.concatenate([-s, s])

    out = np.zeros((128, N_CONST), np.float32)

    def put(name, a):
        out[:, CC[name]:CC[name] + a.shape[1]] = a

    pos = np.arange(L)
    rot = 16
    c, s = table(pos, rot, 500000.0)
    cos_a, sin_a = np.ones((128, L)), np.zeros((128, L))
    for m in (0, 64):
        cos_a[m:m + rot], sin_a[m:m + rot] = c, s
    put("cos_a", cos_a)
    put("sin_a", sin_a)
    rows = np.concatenate([np.full(N_META, -1), np.repeat(np.arange(SEQ // GRID_W), GRID_W)])
    cols = np.concatenate([np.arange(N_META), np.tile(np.arange(GRID_W), SEQ // GRID_W)])
    (cr, sr), (cc, sc) = table(rows, 64, 10000.0), table(cols, 64, 10000.0)
    put("cos_b", np.concatenate([cr, cc]))
    put("sin_b", np.concatenate([sr, sc]))
    c, s = table(pos, 64, 500000.0)
    put("cos_c", np.concatenate([c, c]))
    put("sin_c", np.concatenate([s, s]))
    i = np.arange(128)
    put("ident", np.eye(128))
    put("ones", np.ones((128, 128)))
    put("halves", (i[:, None] // 64 == i[None, :] // 64).astype(np.float32))
    put("swap8", ((i[:, None] ^ 8) == i[None, :]).astype(np.float32))
    put("swap32", ((i[:, None] ^ 32) == i[None, :]).astype(np.float32))
    t = np.concatenate([np.arange(8), np.arange(L - 8, L)])
    for g in range(4):
        w = 2 << g
        n = np.clip(t + w - w // 2, 0, L) - np.clip(t - w // 2, 0, L)
        out[:, CC["edge"] + 16 * g:CC["edge"] + 16 * g + 16] = w / n.astype(np.float64)
    return out


def pack_weights(w_in, w_out, uq, ukv):
    stream = np.zeros((DEPTH * ENTRIES, 128, 2, CHUNK), w_in.dtype)
    for l in range(DEPTH):
        wi = w_in[l].reshape(KT, 128, -1)
        wo = w_out[l].reshape(KT, 128, -1)
        n = l * 2 * ENTRIES

        def add(block):
            nonlocal n
            b = block.transpose(1, 0, 2).reshape(128, -1)
            stream[n // 2, :, n % 2, :b.shape[1]] = b
            n += 1

        for p in range(N_PAIRS):
            kind, i = PAIRS[p]
            if kind == "cqr":
                a, r = OFF["cq"] + 256, OFF["ckr"]
                cols = np.concatenate([wi[:, :, a:a + 128], wi[:, :, r:r + 64], wi[:, :, r:r + 64]], axis=2)
            else:
                a = OFF[kind] + 128 * i
                cols = wi[:, :, a:a + 256]
            for b in range(KT // CK):
                add(cols[CK * b:CK * b + CK])
            if p == LEAD_PAIRS - 1:
                q = uq[l].reshape(3, 128, 4, 192)
                kv = ukv[l].reshape(2, 128, 4, 256)
                add(q[:, :, 0:2, 0:128].reshape(3, 128, 256))
                add(q[:, :, 2:4, 0:128].reshape(3, 128, 256))
                add(q[:, :, :, 128:].reshape(3, 128, 256))
                add(kv[:, :, :, 0:128].reshape(2, 128, 512))
                add(kv[:, :, :, 128:].reshape(2, 128, 512))
                n += 1
        for p in range(O_PAIRS):
            for b in range(KT // CK):
                add(wo[CK * b:CK * b + CK, :, 256 * p:256 * p + 256])
    return stream.reshape(DEPTH * ENTRIES, 128, 2 * CHUNK)


def pack_params(v):
    par = np.zeros((128, DEPTH, N_PAR), np.float32)

    def put(name, a):
        a = a.reshape(DEPTH, -1, 128).transpose(2, 0, 1)
        par[:, :, PC[name]:PC[name] + a.shape[2]] = a

    twice = lambda a: np.concatenate([a, a], axis=1)
    put("norm", v["norm_w"])
    put("aq", twice(v["a_q_norm"]))
    put("ak", twice(v["a_k_norm"]))
    put("sub", v["a_subln"])
    put("bq", v["b_q_norm"])
    put("bk", v["b_k_norm"])
    put("cq", v["c_q_lat_norm"])
    put("ckv", v["c_kv_lat_norm"])
    put("qn", v["c_q_norm"][:, :128])
    put("qr", twice(v["c_q_norm"][:, 128:]))
    put("kn", v["c_k_norm"][:, :128])
    put("kr", twice(v["c_k_norm"][:, 128:]))
    put("dsc", v["d_scale"])
    return par.reshape(128, DEPTH * N_PAR)


def kernel(**inputs):
    import concourse.bacc as _bacc
    from concourse.bass_utils import run_bass_kernel_spmd as _run

    v = {k: np.asarray(a) for k, a in inputs.items()}
    tokens = np.concatenate([v["meta_tokens"], v["x"][0]], axis=0)
    d_w = v["d_w_group"].transpose(2, 0, 1, 3).reshape(128, -1)
    arrays = {
        "xt": np.ascontiguousarray(tokens.reshape(L, KT, 128).transpose(2, 1, 0)),
        "w_stream": pack_weights(v["w_in"], v["w_out"], v["c_w_uq"], v["c_w_ukv"]),
        "params": pack_params(v),
        "lam_rows": np.ascontiguousarray(np.broadcast_to(v["a_lambda"].reshape(1, -1), (128, DEPTH * 256))),
        "consts": np.concatenate([constants(), d_w], axis=1),
    }
    nc = _bacc.Bacc("TRN2", target_bir_lowering=False, num_devices=1)
    args = [nc.dram_tensor(f"{n}_dram", a.shape, mybir.dt.from_np(a.dtype), kind="ExternalInput").ap()
            for n, a in arrays.items()]
    out = nc.dram_tensor("out_dram", (128, KT, SEQ), mybir.dt.float32, kind="ExternalOutput").ap()
    build(nc, *args, out)
    r = _run(nc, [{f"{n}_dram": a for n, a in arrays.items()}], core_ids=[0])
    got = r.results[0]["out_dram"]
    return np.ascontiguousarray(got.transpose(2, 1, 0)).reshape(1, SEQ, D_MODEL)
```

```python
import math
from contextlib import ExitStack

import numpy as np
from concourse import mybir

D_MODEL, SEQ, DEPTH, N_META, GRID_W = 2048, 256, 2, 16, 64
L = N_META + SEQ
EPS = 1e-6
KT = D_MODEL // 128
CK = 4
CHUNK = CK * 256
N_PAIRS = 23
O_PAIRS = D_MODEL // 256
U_CHUNKS = 5
LEAD_PAIRS = 4
SLOTS = 4 * N_PAIRS + U_CHUNKS + 4 * O_PAIRS
ENTRIES = (SLOTS + 1) // 2
RAW, RING, AHEAD = 3, 4, 3
K_BLOCKS = [(0, 128), (128, 128), (256, L - 256)]

OFF = dict(aq=0, ak=512, av=1024, ag=1536, bq=2048, bk=2560, bv=2816, bg=3072, cq=3584, ckv=3968,
           ckr=4224, cg=4288, du=4800, dg=5312)
PAIRS = [("cq", 0), ("ckv", 0), ("cqr", 2), ("cg", 0), ("cg", 2), ("du", 0), ("du", 2),
         ("aq", 0), ("ak", 0), ("av", 0), ("ag", 0), ("aq", 2), ("ak", 2), ("av", 2), ("ag", 2),
         ("bk", 0), ("bv", 0), ("bq", 0), ("bg", 0), ("bq", 2), ("bg", 2), ("dg", 0), ("dg", 2)]

PC = dict(norm=0, aq=16, ak=17, sub=18, bq=19, bk=20, cq=21, ckv=24, qn=26, qr=27, kn=28, kr=29, dsc=30)
N_PAR = 34
N_MATS = 5 * 128
CC = dict(ident=0, ones=128, halves=256, swap8=384, swap32=512, edge=N_MATS,
          **{name: N_MATS + 64 + L * i
             for i, name in enumerate(("cos_a", "sin_a", "cos_b", "sin_b", "cos_c", "sin_c"))})
N_CONST = N_MATS + 64 + 6 * L


def lambda_init(layer):
    return 0.8 - 0.6 * math.exp(-0.3 * layer)


def pair_slot(p):
    return 4 * p + (U_CHUNKS if p >= LEAD_PAIRS else 0)


def first_query(layer):
    return N_META if layer == DEPTH - 1 else 0


def query_tiles(layer):
    q0 = first_query(layer)
    return [(q, min(128, L - q)) for q in range(q0, L, 128)]


OUT_ORDER = (0, 2, 1, 3)
FIRST_STEP = {("c", 0): (5, 3), ("c", 2): (7, 1), ("a", 0): (10, 2), ("a", 1): (12, 1), ("a", 2): (14, 1),
              ("a", 3): (16, 1), ("b", 0): (19, -1), ("b", 2): (21, 0)}
GATE_LATER = {("cg", 0): 5, ("cg", 1): 4, ("cg", 2): 0, ("cg", 3): 2, ("ag", 0): 0, ("ag", 1): 2, ("ag", 2): 2,
              ("ag", 3): 1, ("bg", 0): 0, ("bg", 1): 2, ("bg", 2): 0, ("bg", 3): 1, ("dg", 0): 0, ("dg", 1): 2,
              ("dg", 2): 0, ("dg", 3): 1}


def score_steps(layer):
    n = len(query_tiles(layer))
    first = {key: pair_slot(p) + more for key, (p, more) in FIRST_STEP.items()}
    return [(s0 + 2 * i, b, h, i) for (b, h), s0 in first.items() for i in range(n)]


AT_TENSOR = dict(chunk=0.5, score=0.515, lat_stat=0.595, xsum=0.6, rope_stat=0.6, sub_stat=0.6, mix=0.605, pv=0.61,
                 p_turn=0.863, v_turn=1.817)
AT_SCALAR = dict(rope_fin=-0.166, lat_fin=0.07, mix_out=0.09, lat_pre=0.097, sub_fin=0.1, rope_pre=0.11,
                 y_split=0.205, xscale=0.283, sub_pre=0.439, x_out=0.55, p_out=0.56, gate=0.574, s_exp=0.579,
                 lift=0.6, up_out=0.705, split=0.71, x_square=0.72, y_gate=0.77, lam_exp=0.793, v_out=1.297)
AT_VECTOR = dict(s_max=-0.418, lam_dot=-0.35, sub_fin=-0.345, rope_fin=-0.34, lat_fin=0.055, head_out=0.17,
                 y_split=0.19, pool=0.266, xscale=0.283, gate=0.336, s_scale=0.491, x_out=0.512, rescale=0.55,
                 x_add=0.614, split=0.71, lam_out=0.82, y_gate=1.284)

MOVED = {("split", 1, 56): 0.54, ("lift", 1, 2, 1): 0.49, ("lift", 0, 22, 0): -0.39, ("split", 1, 102): 0.87,
         ("rescale", 0, 20, 1): 1.01, ("split", 1, 101): 0.95}


def make_plan(at_engine):
    plan = []

    def at(slot, stage):
        kind = "y_gate" if stage[:2] == ("y_split", "gate") else stage[0]
        if kind in at_engine:
            plan.append((slot + at_engine[kind] + MOVED.get(stage, 0), len(plan), stage))

    for s in range(AHEAD + 1):
        plan += [(-10 + s, 0, ("split", 0, s)), (-10 + s, 1, ("x_first", 0, s))]
    for g in range(DEPTH * SLOTS):
        at(g, ("chunk", *divmod(g, SLOTS)))
        if AHEAD < g + AHEAD < DEPTH * SLOTS:
            at(g, ("split", *divmod(g + AHEAD, SLOTS)))
    for l in range(DEPTH):
        g0 = l * SLOTS
        if l == 0:
            for c in range(4):
                at(c + 1, ("x_square", l, c))
            for n in range(3):
                at(n + 3, ("x_add", l, n))
            for n, stage in enumerate(("lam_dot", "lam_exp", "lam_out")):
                at(8 + n, (stage, l))
        at(g0 + (2 if l else 6), ("xsum", l))
        at(g0 + (3 if l else 7), ("xscale", l))
        for p, (kind, i0) in enumerate(PAIRS):
            end = g0 + pair_slot(p) + 3
            for j in (0, 1):
                at(end, ("lift", l, p, j))
                at(7 if (l, p) == (0, 0) else end, ("rescale", l, p, j))
                s = end + 1 + j
                if kind in ("aq", "ak", "bq", "bk"):
                    at(s, ("rope_pre", l, kind, i0 + j, j))
                    at(s, ("rope_stat", l, kind, i0 + j))
                    at(s + 1, ("rope_fin", l, kind, i0 + j))
                elif kind in ("av", "bv"):
                    at(s, ("v_turn", l, kind, i0 + j, j))
                    at(s + 1, ("v_out", l, kind, i0 + j))
                elif kind in ("ag", "bg", "cg", "dg"):
                    s = end + 1 + GATE_LATER[(kind, i0 + j)]
                    at(s, ("gate", l, kind, i0 + j, j))
                    if kind == "dg":
                        at(s, ("y_split", "gate", l, kind, i0 + j, j))
                elif kind == "du":
                    at(s, ("pool", l, i0 + j, j))
                    at(s + 1, ("mix", l, i0 + j))
                    at(s + 2, ("mix_out", l, i0 + j))
        s = g0 + pair_slot(3)
        for n, key in enumerate(("cq", "ckv")):
            at(s + n, ("lat_pre", l, key))
            at(s + n, ("lat_stat", l, key))
            at(s + n + 1, ("lat_fin", l, key))
            at(s + n + 1, ("y_split", "lat_fin", l, key))
        at(s + 2, ("rope_pre", l, "kr", 0, None))
        at(s + 2, ("rope_stat", l, "kr", 0))
        at(s + 3, ("rope_fin", l, "kr", 0))
        for c in range(U_CHUNKS):
            at(s + 4 + c, ("up_out", l, c))
        posts = [("qn", 0), ("kn", 0), ("qr", 0), ("qn", 1), ("kn", 1),
                 ("qn", 2), ("kn", 2), ("qr", 1), ("qn", 3), ("kn", 3)]
        for n, (key, i) in enumerate(posts):
            s = g0 + pair_slot(4) + 1 + n
            at(s, ("rope_pre", l, key, i, None))
            at(s, ("rope_stat", l, key, i))
            at(s + 1, ("rope_fin", l, key, i))
        last = len(query_tiles(l)) - 1
        for n, (s, b, h, i) in enumerate(score_steps(l)):
            s += g0
            at(s, ("score", l, n))
            at(s + 1, ("s_max", l, n))
            at(s + 1, ("s_exp", l, n))
            at(s + 1, ("s_scale", l, n))
            at(s + 2, ("p_turn", l, n))
            at(s + 3, ("p_out", l, n))
            at(s + 3, ("pv", l, n))
            if b != "a":
                at(s + 4, ("head_out", l, n))
                at(s + 4, ("y_split", "head_out", l, n))
            elif i == last:
                s = sub_slot(l, n, s + 4)
                at(s, ("sub_pre", l, n))
                at(s, ("sub_stat", l, n))
                at(s + 1, ("sub_fin", l, n))
                at(s + 1, ("y_split", "sub_fin", l, n))
        for n in range(O_PAIRS):
            at(g0 + pair_slot(N_PAIRS) + 4 * n + 3, ("x_out", l, n))
    return [("setup", 0)] + [stage for _, _, stage in sorted(plan)]


def sub_slot(l, n, s):
    taken = set()
    for p, (kind, _) in enumerate(PAIRS):
        if kind in ("aq", "ak", "bq", "bk"):
            taken |= {pair_slot(p) + 4, pair_slot(p) + 5}
    while s - l * SLOTS in taken:
        s += 1
    return s


def build(nc, xt, w_stream, params, lam_rows, consts, out):
    F32, F32R = mybir.dt.float32, mybir.dt.float32r
    ALU, ACT, AX = mybir.AluOpType, mybir.ActivationFunctionType, mybir.AxisListType

    ctx = ExitStack()

    def sb(name, shape, dt=F32):
        return ctx.enter_context(nc.sbuf_tensor(name, shape, dt))

    def bank(name):
        return ctx.enter_context(nc.psum_tensor(name, [128, 512], F32))

    def sem(name):
        return ctx.enter_context(nc.semaphore(name))

    raw = sb("raw", [128, RAW, 2 * CHUNK])
    w_hi = sb("w_hi", [128, RING, CHUNK], F32R)
    w_lo = sb("w_lo", [128, RING, CHUNK], F32R)
    x = sb("x", [128, KT, L])
    h_hi = sb("h_hi", [128, KT, L], F32R)
    h_lo = sb("h_lo", [128, KT, L], F32R)
    y_hi = sb("y_hi", [128, KT, L], F32R)
    y_lo = sb("y_lo", [128, KT, L], F32R)
    con = sb("con", [128, N_CONST])
    par = sb("par", [128, DEPTH * N_PAR])
    q_st = sb("q_st", [128, 4, L])
    k_st = sb("k_st", [128, 4, L])
    v_st = sb("v_st", [128, 3, 4 * 128])
    g_st = sb("g_st", [128, 4, L])
    c_st = sb("c_st", [128, 8, L])
    row = sb("row", [128, 2, L + 16])
    sq = sb("sq", [128, 3, L])
    qw = sb("qw", [128, 2, L])
    rn = sb("rn", [128, L])
    ta = sb("ta", [128, L + 16])
    tb = sb("tb", [128, L + 16])
    gate_e = sb("gate_e", [128, L])
    pooled = sb("pooled", [128, L])
    probs = sb("probs", [128, 2, 2, L])
    p_t = sb("p_t", [128, 2, 3 * 128])
    acc = sb("acc", [128, L])
    rinv = sb("rinv", [128, L])
    d_w = sb("d_w", [128, 4 * 128])
    yt = sb("yt", [128, L])
    stat = sb("stat", [128, 8])
    lam_in = p_t[:, :, :].rearrange("p a b -> p (a b)")[:, 0:DEPTH * 256]
    lam_sum = sb("lam_sum", [128, DEPTH * 2])
    neg_lam = sb("neg_lam", [128, DEPTH])
    sub_w = sb("sub_w", [128, DEPTH])
    eps_c = sb("eps_c", [128, 1])

    dense = [bank("dense0"), bank("dense1")]
    norm_ps, swap_ps = bank("norm_ps"), bank("swap_ps")
    s_ps = [bank("s_ps0"), bank("s_ps1")]
    t_ps, o_ps = bank("t_ps"), bank("o_ps")

    def const(name, n=L):
        return con[:, CC[name]:CC[name] + n]

    ident, ones, halves = const("ident", 128), const("ones", 128), const("halves", 128)
    swap = {"a": const("swap8", 128), "b": const("swap32", 128), "c": const("swap32", 128)}

    def pcol(l, name, i=0):
        c = l * N_PAR + PC[name] + i
        return par[:, c:c + 1]

    LATENT = {"cq": (0, 3), "ckv": (3, 2)}
    SCALE = {"a": 64 ** -0.5, "b": 128 ** -0.5, "c": 192 ** -0.5}

    def turned(m, b, nk, nq):
        if m == 0:
            return t_ps[0:nk, 128 * b:128 * b + nq]
        return o_ps[0:nk, 256 + 128 * b:256 + 128 * b + nq] if b < 2 else t_ps[0:nk, 384:384 + nq]

    def square_store(c):
        return (q_st, k_st, g_st)[c][:, :, :] if c < 3 else probs[:, :, :, :].rearrange("p a b t -> p (a b) t")

    def pair_view(t, n):
        return t[:, 0:256].rearrange("p (m q) -> p m q", m=2)[:, :, 0:n]

    s_const, s_par, s_lam, s_dw = sem("s_const"), sem("s_par"), sem("s_lam"), sem("s_dw")
    s_x = [sem(f"s_x{i}") for i in range(4)]
    s_first = [sem(f"s_first{i}") for i in range(4)]
    s_tab = sem("s_tab")
    s_raw = [sem(f"s_raw{i}") for i in range(RAW)]
    s_stored = sem("s_stored")
    hi_ready, lo_ready, chunk_done = sem("hi_ready"), sem("lo_ready"), sem("chunk_done")
    tile_done = sem("tile_done")
    lifted = sem("lifted")
    scaled = sem("scaled")
    up_taken = sem("up_taken")
    xt_taken = sem("xt_taken")
    sq_x = sem("sq_x")
    h_hi_ready, h_ready = sem("h_hi_ready"), sem("h_ready")
    acc_ready = sem("acc_ready")
    pre_done, stat_done, rn_ready, fin_done = sem("pre_done"), sem("stat_done"), sem("rn_ready"), sem("fin_done")
    turned_v, v_ready = sem("turned_v"), sem("v_ready")
    gate_exp, gate_done = sem("gate_exp"), sem("gate_done")
    pooled_ready, mixed_ps, mixed = sem("pooled_ready"), sem("mixed_ps"), sem("mixed")
    scores_ready, bias_ready, exp_done, w_ready = (sem("scores_ready"), sem("bias_ready"),
                                                   sem("exp_done"), sem("w_ready"))
    turned_p, pt_ready, pv_done, o_taken = sem("turned_p"), sem("pt_ready"), sem("pv_done"), sem("o_taken")
    y_hi_done, y_ready = sem("y_hi_done"), sem("y_ready")
    act_own, dve_own = sem("act_own"), sem("dve_own")
    lam_ready, lam_exp = sem("lam_ready"), sem("lam_exp")

    UP_TILES = 13

    def up_tiles(c):
        return [2, 2, 2, 4, 3][c]

    def up_no(c, j):
        return sum(up_tiles(i) for i in range(c)) + j + 1

    def chunk_size(s):
        kind, a, _ = chunk_kind(s)
        return 768 if kind == "up" and a < 3 else CHUNK

    def chunk_kind(s):
        u0 = pair_slot(3) + 4
        if u0 <= s < u0 + U_CHUNKS:
            return "up", s - u0, 0
        if s >= pair_slot(N_PAIRS):
            return ("out", *divmod(s - pair_slot(N_PAIRS), 4))
        return ("in", *divmod(s - (U_CHUNKS if s > u0 else 0), 4))

    u_end = pair_slot(3) + 4 + U_CHUNKS

    def entry(l, s):
        n = s + (1 if s >= u_end else 0)
        return l * ENTRIES + n // 2, n % 2

    n_taken = {"in": 0, "up": 0, "out": 0}
    freed_by, tile_no = {}, {}
    n_tile = 0
    for l in range(DEPTH):
        for s in range(SLOTS):
            kind, a, b = chunk_kind(s)
            if kind == "up":
                members = [(kind, a, j) for j in range(up_tiles(a))]
            elif b == 3:
                members = [(kind, a, j) for j in (0, 1)]
            else:
                members = []
            for m in members:
                n_taken[m[0]] += 1
                tile_no[(l, *m)] = n_tile
                freed_by[n_tile] = (m[0], n_taken[m[0]])
                n_tile += 1
    taken = {"in": lifted, "up": up_taken, "out": xt_taken}

    steps = [(l, n, *st) for l in range(DEPTH) for n, st in enumerate(score_steps(l))]
    step_no = {(l, n): i for i, (l, n, *_) in enumerate(steps)}

    def last_step_using(l, branch, store, i):
        best = 0
        for k, (ll, n, s, b, h, qi) in enumerate(steps):
            if ll != l or b != branch:
                continue
            if b == "a":
                used = {h}
            elif b == "b" and store in ("k", "v"):
                used = {h // 2}
            else:
                used = {h, h + 1}
            if i in used:
                best = k + 1
        return best

    before = {"a": "c", "b": "a", "c": "b"}

    def store_free(l, branch, store, i):
        prev = before[branch]
        if prev == "b":
            return last_step_using(l - 1, prev, store, i) if l else 0
        return last_step_using(l, prev, store, i)

    norm_order, swap_order, pre_no, fin_no, gate_no = {}, {}, {}, {}, {}
    fins_before, scaled_no, v_no, y_count = {}, {}, {}, {}
    tensor_plan, scalar_plan, vector_plan = make_plan(AT_TENSOR), make_plan(AT_SCALAR), make_plan(AT_VECTOR)
    for stg in tensor_plan:
        if stg[0] in ("rope_stat", "lat_stat", "sub_stat", "xsum"):
            norm_order[stg] = len(norm_order)
        if stg[0] in ("v_turn", "mix") or (stg[0] == "rope_stat" and stg[2] not in ("qn", "kn")):
            swap_order[stg] = len(swap_order)
    for stg in scalar_plan:
        if stg[0] in ("rope_pre", "lat_pre", "sub_pre"):
            pre_no[stg[:4] if stg[0] == "rope_pre" else stg] = len(pre_no) + 1
        if stg[0] == "v_out":
            v_no[stg[1:]] = len(v_no) + 1
    for stg in vector_plan:
        fins_before[stg] = len(fin_no)
        if stg[0] in ("rope_fin", "lat_fin", "sub_fin"):
            fin_no[stg] = len(fin_no) + 1
        if stg[0] == "gate":
            gate_no[stg] = len(gate_no) + 1
        if stg[0] == "rescale":
            scaled_no[stg[1:]] = len(scaled_no) + 1
    n_scaled = {(l, *PAIRS[p], j): n for (l, p, j), n in scaled_no.items()}
    norm_list = list(norm_order)

    def parity(*stage):
        return norm_order[stage] % 2

    def halves_free(*stage):
        n = norm_order[stage]
        lat = lambda k: k >= 0 and norm_list[k][0] == "lat_stat"
        stats = n if stage[0] == "lat_stat" or lat(n - 1) else n - 1
        fins = 0
        for m in range(n - 1):
            other = norm_list[m]
            if other[0] != "xsum":
                fins = max(fins, fin_no[(other[0].replace("stat", "fin"), *other[1:])])
        return stats, fins

    swap_list = list(swap_order)
    takes_swap = {"rope_stat": fin_done, "v_turn": v_ready, "mix": mixed}

    def swap_taken_value(stage):
        if stage[0] == "rope_stat":
            return fin_no[("rope_fin", *stage[1:])]
        if stage[0] == "v_turn":
            return v_no[stage[1:4]]
        return 4 * stage[1] + stage[2] + 1

    def scaled_of(l, kind, i):
        if kind == "kr":
            return n_scaled[(l, "cqr", 2, 1)]
        return next(n for (ll, k, i0, j), n in n_scaled.items() if ll == l and k == kind and i0 + j == i)

    rope = {"aq": ("a", 64), "ak": ("a", 64), "bq": ("b", 128), "bk": ("b", 128), "kr": ("c", 64),
            "qr": ("c", 64), "qn": (None, 128), "kn": (None, 128)}

    def rope_source(key, i, j):
        if j is not None:
            return row[:, j, 8:8 + L]
        return rope_target(key, i)

    def rope_target(key, i):
        if key in ("aq", "bq", "qn"):
            return q_st[:, i, :]
        if key in ("ak", "bk", "kn"):
            return k_st[:, i, :]
        return c_st[:, 5, :] if key == "kr" else c_st[:, 6 + i, :]

    def rope_from(l, key):
        return first_query(l) if key in ("aq", "bq", "qn", "qr") else 0

    def gate_from(l):
        return first_query(l)

    def tile_from(l, kind):
        return first_query(l) if kind in ("aq", "bq", "ag", "bg", "cg", "dg") else 0

    def uses_row(kind):
        return kind not in ("cq", "ckv", "cqr")

    def tile_place(l, p, j):
        kind = PAIRS[p][0]
        if uses_row(kind):
            return row[:, j, 8 + tile_from(l, kind):8 + L]
        return c_st[:, {"cq": j, "ckv": 3 + j, "cqr": (2, 5)[j]}[kind], :]

    gates_of_layer = len(gate_no) // DEPTH

    def previous_row(l, p):
        while True:
            p -= 1
            if p < 0:
                l, p = l - 1, N_PAIRS - 1
            if l < 0:
                return None
            if uses_row(PAIRS[p][0]):
                return l, p

    def y_tile(*source):
        n = y_count[source]
        if source[0] == "lat_fin":
            k0, m = LATENT[source[2]]
            return n, lambda y: y[:, k0:k0 + m, :], c_st[:, k0:k0 + m, :], (fin_done, fin_no[source])
        l = source[1]
        t0 = first_query(l)
        if source[0] == "gate":
            r = rows_of("d", source[3])
            return n, lambda y: y[:, r, t0:L], yt[:, t0:L], (gate_done, gate_no[source])
        _, b, h, i = score_steps(l)[source[2]]
        r = rows_of(b, h)
        if source[0] == "sub_fin":
            return n, lambda y: y[:, r, t0:L], yt[:, t0:L], (fin_done, fin_no[source])
        q, nq = query_tiles(l)[i]
        return (n, lambda y: y[:, r:r + 2, q:q + nq], pair_view(yt, nq),
                (o_taken, o_before[step_no[(l, source[2])]] + 1))

    o_before, n_o = [], 0
    for k, (l, n, _, b, h, i) in enumerate(steps):
        o_before.append(n_o)
        n_o += 1 if b != "a" or i == len(query_tiles(l)) - 1 else 0

    def needs_of(branch, h):
        return {"a": [("aq", h), ("ak", h)],
                "b": [("bq", h), ("bq", h + 1), ("bk", h // 2)],
                "c": [("qn", h), ("qn", h + 1), ("kn", h), ("kn", h + 1), ("qr", h // 2), ("kr", 0)]}[branch]

    def rows_of(kind, i):
        return {"a": 0, "b": 4, "c": 8, "d": 12}[kind] + i

    n_y = 0
    for stg in vector_plan:
        if stg[0] != "y_split":
            continue
        stg = stg[1:]
        l = stg[1]
        if stg[0] == "lat_fin":
            n_y += 1
            y_count[(l, stg[2])] = n_y
            y_count[stg] = n_y
        elif stg[0] in ("head_out", "sub_fin"):
            n_y += 1
            y_count[(l, "abc".index(score_steps(l)[stg[2]][1]))] = n_y
            y_count[stg] = n_y
        else:
            n_y += 1
            y_count[(l, 3, stg[3])] = n_y
            y_count[stg] = n_y

    tile_sem, n_mid, g = {}, 0, 0
    for l in range(DEPTH):
        for s in range(SLOTS):
            g += 1
            kind, a, b = chunk_kind(s)
            n = up_tiles(a) if kind == "up" else (2 if b == 3 else 0)
            for j in range(n):
                if j < n - 1:
                    n_mid += 1
                    tile_sem[(l, kind, a, j)] = (tile_done, n_mid)
                else:
                    tile_sem[(l, kind, a, j)] = (chunk_done, g)

    def wait_tile(eng, l, kind, a, j):
        which, n = tile_sem[(l, kind, a, j)]
        eng.wait_ge(which, n)
        return dense[tile_no[(l, kind, a, j)] % 2]

    block = ctx.enter_context(nc.Block())

    @block.sync
    def _(sp):
        for c in range(4):
            at = slice(CHUNK * (c % 2), CHUNK * (c % 2) + CHUNK)
            sp.dma_start(raw[:, c // 2, at], w_stream[c // 2, :, at]).then_inc(s_first[c], 16)
            if c == 0:
                sp.dma_start(par[:, :], params).then_inc(s_par, 16)
            sp.dma_start(x[:, 4 * c:4 * c + 4, :], xt[:, 4 * c:4 * c + 4, :]).then_inc(s_x[c], 16)
        for e in range(2, DEPTH * ENTRIES):
            if e >= RAW:
                l, n = divmod(e - RAW, ENTRIES)
                s_last = 2 * n + 1 - (1 if 2 * n + 1 >= u_end else 0)
                if 2 * n + 1 == u_end:
                    s_last = u_end - 1
                sp.wait_ge(lo_ready, l * SLOTS + s_last + 1)
            if e % ENTRIES == 0 and e:
                l = e // ENTRIES
                sp.wait_ge(mixed_ps, 4 * l)
                sp.dma_start(d_w[:, :], consts[:, N_CONST + 512 * l:N_CONST + 512 * l + 512]).then_inc(s_dw, 16)
            sp.dma_start(raw[:, e % RAW, :], w_stream[e, :, :]).then_inc(s_raw[e % RAW], 16)
            if e == 2:
                sp.dma_start(con[:, 0:N_MATS], consts[:, 0:N_MATS]).then_inc(s_const, 16)
            if e == 3:
                sp.dma_start(con[:, N_MATS:N_CONST], consts[:, N_MATS:N_CONST]).then_inc(s_tab, 16)
                sp.dma_start(lam_in, lam_rows).then_inc(s_lam, 16)
                sp.dma_start(d_w[:, :], consts[:, N_CONST:N_CONST + 512]).then_inc(s_dw, 16)
        q0 = first_query(DEPTH - 1)
        for n in range(O_PAIRS):
            sp.wait_ge(xt_taken, 2 * O_PAIRS * (DEPTH - 1) + 2 * n + 2)
            sp.dma_start(out[:, 2 * n:2 * n + 2, :], x[:, 2 * n:2 * n + 2, q0:L]).then_inc(s_stored, 16)
        sp.wait_ge(s_stored, 16 * O_PAIRS)

    @block.tensor
    def _(pe):
        def three(ps, whi, wlo, xhi, xlo, first, last):
            nc.tensor.matmul(ps, whi, xhi, start=first, stop=False)
            nc.tensor.matmul(ps, whi, xlo, start=False, stop=False)
            return nc.tensor.matmul(ps, wlo, xhi, start=False, stop=last)

        def bank_for(tile):
            if tile >= 2:
                kind, n = freed_by[tile - 2]
                pe.wait_ge(taken[kind], n)
            return dense[tile % 2]

        def chunk(l, s):
            kind, a, b = chunk_kind(s)
            g = l * SLOTS + s
            pe.wait_ge(lo_ready, g + 1)
            hi, lo = w_hi[:, g % RING, :], w_lo[:, g % RING, :]
            if kind == "up":
                mm = up_chunk(l, a, hi, lo)
            else:
                xhi, xlo = (h_hi, h_lo) if kind == "in" else (y_hi, y_lo)
                t0 = tile_from(l, PAIRS[a][0]) if kind == "in" else first_query(l)
                for j in (0, 1):
                    tile = tile_no[(l, kind, a, j)]
                    ps = bank_for(tile) if b == 0 else dense[tile % 2]
                    for k in range(CK):
                        kt = CK * (OUT_ORDER[b] if kind == "out" else b) + k
                        if a == 0 and j == 0 and kind == "in":
                            pe.wait_ge(h_ready, KT * l + kt + 1)
                        if a == 0 and j == 0 and kind == "out":
                            if OUT_ORDER[b] == 3:
                                pe.wait_ge(y_ready, y_count[(l, 3, k)])
                            elif k == 0:
                                pe.wait_ge(y_ready, y_count[(l, OUT_ORDER[b])])
                        c = 256 * k + 128 * j
                        mm = three(ps[:, 0:L - t0], hi[:, c:c + 128], lo[:, c:c + 128],
                                   xhi[:, kt, t0:L], xlo[:, kt, t0:L], b + k == 0, (b, k) == (3, CK - 1))
                    if b == 3 and j == 0:
                        mm.then_inc(tile_done, 1)
            mm.then_inc(chunk_done, 1)

        def up_chunk(l, c, hi, lo):
            if c == 0:
                pe.wait_ge(y_ready, y_count[(l, "cq")])
            if c == 3:
                pe.wait_ge(y_ready, y_count[(l, "ckv")])
            q0 = first_query(l)
            for j in range(up_tiles(c)):
                ps = bank_for(tile_no[(l, "up", c, j)])
                if c < 3:
                    for k in range(3):
                        w = slice(256 * k + 128 * j, 256 * k + 128 * j + 128)
                        mm = three(ps[:, 0:L - q0], hi[:, w], lo[:, w],
                                   y_hi[:, k, q0:L], y_lo[:, k, q0:L], k == 0, k == 2)
                elif c == 3:
                    for k in range(2):
                        w = slice(512 * k + 128 * j, 512 * k + 128 * j + 128)
                        mm = three(ps[:, 0:L], hi[:, w], lo[:, w],
                                   y_hi[:, 3 + k, :], y_lo[:, 3 + k, :], k == 0, k == 1)
                else:
                    t, n = K_BLOCKS[j]
                    for k in range(2):
                        w = slice(512 * k, 512 * k + 512)
                        mm = three(ps[0:n, :], y_hi[:, 3 + k, t:t + n], y_lo[:, 3 + k, t:t + n],
                                   hi[:, w], lo[:, w], k == 0, k == 1)
                if j < up_tiles(c) - 1:
                    mm.then_inc(tile_done, 1)
            return mm

        def norm_free(*stage):
            n = norm_order[stage]
            if n:
                pe.wait_ge(rn_ready, n)

        def swap_free(*stage):
            n = swap_order[stage]
            if n:
                prev = swap_list[n - 1]
                pe.wait_ge(takes_swap[prev[0]], swap_taken_value(prev))

        def xsum(l):
            pe.wait_ge(acc_ready, 1 + KT * l)
            pe.wait_ge(s_const, 16)
            norm_free("xsum", l)
            nc.tensor.matmul(norm_ps[:, 0:L], ones, acc[:, :], start=True, stop=True).then_inc(stat_done, 1)

        def rope_stat(l, key, i):
            branch, width = rope[key]
            t0 = rope_from(l, key)
            pe.wait_ge(pre_done, pre_no[("rope_pre", l, key, i)])
            norm_free("rope_stat", l, key, i)
            sums = nc.tensor.matmul(norm_ps[:, t0:L], halves if width == 64 else ones,
                                    sq[:, parity("rope_stat", l, key, i), t0:L],
                                    start=True, stop=True)
            if branch:
                swap_free("rope_stat", l, key, i)
                sums = nc.tensor.matmul(swap_ps[:, t0:L], swap[branch],
                                        qw[:, parity("rope_stat", l, key, i), t0:L], start=True, stop=True)
            sums.then_inc(stat_done, 1)

        def lat_stat(l, key):
            pe.wait_ge(pre_done, pre_no[("lat_pre", l, key)])
            norm_free("lat_stat", l, key)
            n = 3 if key == "cq" else 2
            for k in range(n):
                mm = nc.tensor.matmul(norm_ps[:, 0:L], ones, sq[:, k, :], start=k == 0, stop=k == n - 1)
            mm.then_inc(stat_done, 1)

        def v_turn(l, kind, i, j):
            pe.wait_ge(scaled, scaled_of(l, kind, i))
            swap_free("v_turn", l, kind, i, j)
            for b, (t, n) in enumerate(K_BLOCKS):
                mm = nc.tensor.transpose(swap_ps[0:n, 128 * b:128 * b + 128], row[:, j, 8 + t:8 + t + n], ident)
            mm.then_inc(turned_v, 1)

        def mix(l, g):
            pe.wait_ge(pooled_ready, 4 * l + g + 1)
            if g == 0:
                pe.wait_ge(s_dw, 16 * (l + 1))
            swap_free("mix", l, g)
            nc.tensor.matmul(swap_ps[:, 0:L], d_w[:, 128 * g:128 * g + 128], pooled[:, :],
                             start=True, stop=True).then_inc(mixed_ps, 1)

        def score(l, n):
            _, branch, h, i = score_steps(l)[n]
            q, nq = query_tiles(l)[i]
            k = step_no[(l, n)]
            for key, hh in needs_of(branch, h):
                pe.wait_ge(fin_done, fin_no[("rope_fin", l, key, hh)])
            if k:
                pe.wait_ge(exp_done, 2 * k)
            for m in (0, 1):
                ps = s_ps[m][0:nq, 0:L]
                if branch == "a":
                    half = slice(64 * m, 64 * m + 64)
                    mm = nc.tensor.matmul(ps, q_st[half, h, q:q + nq], k_st[half, h, :], start=True, stop=True)
                elif branch == "b":
                    mm = nc.tensor.matmul(ps, q_st[:, h + m, q:q + nq], k_st[:, h // 2, :], start=True, stop=True)
                else:
                    half = slice(64 * m, 64 * m + 64)
                    nc.tensor.matmul(ps, q_st[:, h + m, q:q + nq], k_st[:, h + m, :], start=True, stop=False)
                    mm = nc.tensor.matmul(ps, c_st[half, 6 + h // 2, q:q + nq], c_st[half, 5, :],
                                          start=False, stop=True)
            mm.then_inc(scores_ready, 1)

        def p_turn(l, n):
            _, branch, h, i = score_steps(l)[n]
            q, nq = query_tiles(l)[i]
            k = step_no[(l, n)]
            pe.wait_ge(w_ready, k + 1)
            if k:
                pe.wait_ge(pt_ready, k)
            for m in range(1 if branch == "a" else 2):
                if m and o_before[k]:
                    pe.wait_ge(o_taken, o_before[k])
                for b, (t, nk) in enumerate(K_BLOCKS):
                    mm = nc.tensor.transpose(turned(m, b, nk, nq),
                                             probs[0:nq, k % 2, m, t:t + nk], ident[0:nq, 0:nq])
            mm.then_inc(turned_p, 1)

        def pv(l, n):
            _, branch, h, i = score_steps(l)[n]
            q, nq = query_tiles(l)[i]
            k = step_no[(l, n)]
            pe.wait_ge(pt_ready, k + 1)
            if branch == "c":
                pe.wait_ge(up_taken, UP_TILES * (l + 1))
            else:
                pe.wait_ge(v_ready, v_no[(l, "av", h) if branch == "a" else (l, "bv", h // 2)])
            if o_before[k]:
                pe.wait_ge(o_taken, o_before[k])
            for m in range(1 if branch == "a" else 2):
                vh = h // 2 if branch == "b" else h + m
                c = q if branch == "a" else 128 * m
                for b, (t, nk) in enumerate(K_BLOCKS):
                    mm = nc.tensor.matmul(o_ps[:, c:c + nq], v_st[0:nk, b, 128 * vh:128 * vh + 128],
                                          p_t[0:nk, m, 128 * b:128 * b + nq], start=b == 0, stop=b == 2)
            mm.then_inc(pv_done, 1)

        def sub_stat(l, n):
            pe.wait_ge(pre_done, pre_no[("sub_pre", l, n)])
            norm_free("sub_stat", l, n)
            t0 = first_query(l)
            nc.tensor.matmul(norm_ps[:, t0:L], ones, sq[:, parity("sub_stat", l, n), t0:L],
                             start=True, stop=True).then_inc(stat_done, 1)

        run = dict(chunk=chunk, xsum=xsum, rope_stat=rope_stat, lat_stat=lat_stat, v_turn=v_turn, mix=mix,
                   score=score, p_turn=p_turn, pv=pv, sub_stat=sub_stat)
        for stage, *what in tensor_plan:
            if stage in run:
                run[stage](*what)

    @block.scalar
    def _(act):
        own = [0]

        def link(ins):
            own[0] += 1
            ins.then_inc(act_own, 1)
            act.wait_ge(act_own, own[0])

        def signal(ins, which, n):
            ins.then_inc(which, 1)
            act.wait_ge(which, n)

        def setup(_):
            nc.scalar.preload_act_table_set("natural_log_exp_and_others")

        def x_first(_, c):
            if c == 0:
                act.wait_ge(s_par, 16)
            act.wait_ge(s_x[c], 16)
            for kt in range(4 * c, 4 * c + 4):
                x_hi(0, kt)

        def x_square(l, c):
            signal(nc.scalar.activation(square_store(c), x[:, 4 * c:4 * c + 4, :], ACT.Square), sq_x, c + 1)

        def lambda_exp(_):
            act.wait_ge(lam_ready, 1)
            signal(nc.scalar.activation(lam_sum[:, :], lam_sum[:, :], ACT.Exp), lam_exp, 1)

        def x_tile(l, kt):
            n = KT * (l - 1) + kt
            act.wait_ge(acc_ready, max(1, n))
            signal(nc.scalar.activation(sq[:, kt % 2, :], x[:, kt, :], ACT.Square), sq_x, 4 + n + 1)
            x_hi(l, kt)

        def x_hi(l, kt):
            signal(nc.scalar.activation(h_hi[:, kt, :], x[:, kt, :], ACT.Copy, scale=pcol(l, "norm", kt)),
                   h_hi_ready, KT * l + kt + 1)

        def x_out(l, n):
            if l < DEPTH - 1:
                for kt in (2 * n, 2 * n + 1):
                    act.wait_ge(xt_taken, KT * l + kt + 1)
                    x_tile(l + 1, kt)

        def split(l, s):
            g = l * SLOTS + s
            e, half = entry(l, s)
            n = chunk_size(s)
            if e < 2:
                act.wait_ge(s_first[s], 16)
            else:
                act.wait_ge(s_raw[e % RAW], 16 * (e // RAW + (e % RAW > 1)))
            if g >= RING:
                act.wait_ge(chunk_done, g - RING + 1)
            signal(nc.scalar.activation(w_hi[:, g % RING, 0:n], raw[:, e % RAW, CHUNK * half:CHUNK * half + n],
                                        ACT.Copy), hi_ready, g + 1)

        def lift(l, p, j):
            kind, i0 = PAIRS[p]
            ps = wait_tile(act, l, "in", p, j)
            if not uses_row(kind):
                if l:
                    act.wait_ge(gate_done, gates_of_layer * l)
                if kind == "cqr" and j and l:
                    act.wait_ge(scores_ready, last_step_using(l - 1, "c", "k", 3))
            else:
                prev = previous_row(l, p)
                if prev:
                    pk, pi = PAIRS[prev[1]]
                    i = pi + j
                    if pk in ("av", "bv"):
                        act.wait_ge(turned_v, v_no[(prev[0], pk, i)])
                    elif pk == "du":
                        act.wait_ge(pooled_ready, 4 * prev[0] + i + 1)
                    elif pk[1] == "g":
                        act.wait_ge(gate_done, gate_no[("gate", prev[0], pk, i, j)])
            signal(nc.scalar.activation(tile_place(l, p, j), ps[:, 0:L - tile_from(l, kind)], ACT.Copy), lifted,
                   scaled_no[(l, p, j)])

        def up_out(l, c):
            for j in range(up_tiles(c)):
                ps = wait_tile(act, l, "up", c, j)
                q0 = first_query(l)
                if c < 2:
                    i, out_ = 2 * c + j, q_st[:, 2 * c + j, q0:L]
                    free = (scores_ready, store_free(l, "c", "q", i))
                elif c == 2:
                    out_, free = c_st[:, 6 + j, q0:L], (scores_ready, store_free(l, "c", "q", j))
                elif c == 3:
                    out_, free = k_st[:, j, :], (scores_ready, store_free(l, "c", "k", j))
                else:
                    n = K_BLOCKS[j][1]
                    out_, free = v_st[0:n, j, :], (pv_done, store_free(l, "c", "v", 3))
                if free[1]:
                    act.wait_ge(*free)
                src = ps[0:K_BLOCKS[j][1], :] if c == 4 else ps[:, 0:L - q0] if c < 3 else ps[:, 0:L]
                signal(nc.scalar.activation(out_, src, ACT.Copy), up_taken, UP_TILES * l + up_no(c, j))

        def buffers_free(*stage):
            stats, fins = halves_free(*stage)
            if stats > 0:
                act.wait_ge(stat_done, stats)
            if fins:
                act.wait_ge(fin_done, fins)

        def rope_pre(l, key, i, j):
            branch, width = rope[key]
            t0 = rope_from(l, key)
            if key in ("qn", "kn", "qr"):
                pass
            else:
                act.wait_ge(scaled, scaled_of(l, key, i))
            buffers_free("rope_stat", l, key, i)
            half = parity("rope_stat", l, key, i)
            src = rope_source(key, i, j)[:, t0:L]
            square = nc.scalar.activation(sq[:, half, t0:L], src, ACT.Square)
            if branch:
                link(square)
                square = nc.scalar.activation(qw[:, half, t0:L], src, ACT.Copy, scale=pcol(l, key))
            signal(square, pre_done, pre_no[("rope_pre", l, key, i)])

        def lat_pre(l, key):
            k0, n = LATENT[key]
            act.wait_ge(scaled, scaled_no[(l, 2, 0) if key == "cq" else (l, 1, 1)])
            buffers_free("lat_stat", l, key)
            signal(nc.scalar.activation(sq[:, 0:n, :], c_st[:, k0:k0 + n, :], ACT.Square), pre_done,
                   pre_no[("lat_pre", l, key)])

        def sub_pre(l, n):
            t0 = first_query(l)
            act.wait_ge(pv_done, step_no[(l, n)] + 1)
            buffers_free("sub_stat", l, n)
            signal(nc.scalar.activation(sq[:, parity("sub_stat", l, n), t0:L], o_ps[:, t0:L], ACT.Square), pre_done,
                   pre_no[("sub_pre", l, n)])

        def inverse_root(stat_stage, fin_stage, width, t0, out_):
            n = norm_order[stat_stage]
            act.wait_ge(stat_done, n + 1)
            if fins_before[fin_stage]:
                act.wait_ge(fin_done, fins_before[fin_stage])
            link(nc.scalar.activation(rn[:, t0:L], norm_ps[:, t0:L], ACT.Ln, scale=1.0 / width, bias=eps_c[:, 0:1]))
            signal(nc.scalar.activation(out_, rn[:, t0:L], ACT.Exp, scale=-0.5), rn_ready, n + 1)

        def xscale(l):
            if l:
                act.wait_ge(scaled, 2 * N_PAIRS * l)
            inverse_root(("xsum", l), ("xscale", l), D_MODEL, 0, rinv[:, :])

        def rope_fin(l, key, i):
            t0 = rope_from(l, key)
            inverse_root(("rope_stat", l, key, i), ("rope_fin", l, key, i), rope[key][1], t0, rn[:, t0:L])

        def lat_fin(l, key):
            k0, n = LATENT[key]
            inverse_root(("lat_stat", l, key), ("lat_fin", l, key), 128 * n, 0, rn[:, :])

        def sub_fin(l, n):
            t0 = first_query(l)
            inverse_root(("sub_stat", l, n), ("sub_fin", l, n), 128, t0, rn[:, t0:L])

        def y_split(*source):
            n, out_, src, ready = y_tile(*source)
            l = source[1]
            act.wait_ge(*ready)
            if source[0] != "lat_fin":
                act.wait_ge(chunk_done, SLOTS * l + u_end)
            elif l:
                act.wait_ge(chunk_done, SLOTS * l)
            signal(nc.scalar.activation(out_(y_hi), src, ACT.Copy), y_hi_done, n)

        def gate(l, kind, i, j):
            t0 = gate_from(l)
            n = gate_no[("gate", l, kind, i, j)]
            act.wait_ge(scaled, scaled_of(l, kind, i))
            if n > 1:
                act.wait_ge(gate_done, n - 1)
            signal(nc.scalar.activation(gate_e[:, t0:L], row[:, j, 8 + t0:8 + L], ACT.Exp, scale=-1.0), gate_exp, n)

        def v_out(l, kind, i):
            act.wait_ge(turned_v, v_no[(l, kind, i)])
            free = store_free(l, kind[0], "v", i)
            if free:
                act.wait_ge(pv_done, free)
            c = slice(128 * i, 128 * i + 128)
            link(nc.scalar.activation(v_st[:, 0:2, c], swap_ps[:, 0:256].rearrange("p (b d) -> p b d", b=2),
                                      ACT.Copy))
            signal(nc.scalar.activation(v_st[0:16, 2, c], swap_ps[0:16, 256:384], ACT.Copy), v_ready,
                   v_no[(l, kind, i)])

        def mix_out(l, g):
            n = 4 * l + g + 1
            act.wait_ge(mixed_ps, n)
            act.wait_ge(y_ready, y_count[(l, "ckv")])
            signal(nc.scalar.activation(c_st[:, g, :], swap_ps[:, 0:L], ACT.Copy, scale=pcol(l, "dsc", g)), mixed, n)

        def s_exp(l, n):
            k = step_no[(l, n)]
            _, b, h, i = score_steps(l)[n]
            nq = query_tiles(l)[i][1]
            act.wait_ge(bias_ready, k + 1)
            if k >= 2:
                act.wait_ge(turned_p, k - 1)
            for m in (0, 1):
                signal(nc.scalar.activation(probs[0:nq, k % 2, m, :], s_ps[m][0:nq, 0:L], ACT.Exp,
                                            bias=stat[0:nq, 2 + m:3 + m], scale=SCALE[b],
                                            accum_out=stat[0:nq, 4 + m:5 + m]), exp_done, 2 * k + m + 1)

        def p_out(l, n):
            k = step_no[(l, n)]
            _, b, h, i = score_steps(l)[n]
            nq = query_tiles(l)[i][1]
            act.wait_ge(turned_p, k + 1)
            if k:
                act.wait_ge(pv_done, k)
            for m in range(1 if b == "a" else 2):
                ps = (t_ps[:, 0:256], o_ps[:, 256:512])[m]
                link(nc.scalar.activation(p_t[:, m, 0:256].rearrange("p (b q) -> p b q", b=2)[:, :, 0:nq],
                                          ps.rearrange("p (b q) -> p b q", b=2)[:, :, 0:nq], ACT.Copy))
                tail = nc.scalar.activation(p_t[0:16, m, 256:256 + nq], turned(m, 2, 16, nq), ACT.Copy)
                if m == 0 and b != "a":
                    link(tail)
            signal(tail, pt_ready, k + 1)

        run = dict(setup=setup, lift=lift, x_first=x_first, x_square=x_square, lam_exp=lambda_exp,
                   x_out=x_out, split=split,
                   up_out=up_out, rope_pre=rope_pre,
                   lat_pre=lat_pre, sub_pre=sub_pre, xscale=xscale, rope_fin=rope_fin, lat_fin=lat_fin,
                   sub_fin=sub_fin, y_split=y_split, gate=gate, v_out=v_out, mix_out=mix_out, s_exp=s_exp,
                   p_out=p_out)
        for stage, *what in scalar_plan:
            if stage in run:
                run[stage](*what)

    @block.vector
    def _(dve):
        own = [0]

        def link(ins):
            own[0] += 1
            ins.then_inc(dve_own, 1)
            dve.wait_ge(dve_own, own[0])

        def signal(ins, which, n):
            ins.then_inc(which, 1)
            dve.wait_ge(which, n)

        def setup(_):
            link(nc.vector.memset(eps_c[:, :], EPS))
            link(nc.vector.memset(row[:, :, :], 0.0))

        def x_first(_, c):
            dve.wait_ge(s_x[c], 16)
            if c == 0:
                dve.wait_ge(s_par, 16)
            for kt in range(4 * c, 4 * c + 4):
                x_lo(0, kt)

        def x_add(l, n):
            a = square_store(0)
            dve.wait_ge(sq_x, n + 2)
            link(nc.vector.tensor_tensor(a, a, square_store(n + 1), ALU.add))
            if n < 2:
                return
            link(nc.vector.tensor_tensor(a[:, 0:2, :], a[:, 0:2, :], a[:, 2:4, :], ALU.add))
            signal(nc.vector.tensor_tensor(acc[:, :], a[:, 0, :], a[:, 1, :], ALU.add), acc_ready, 1)

        def lam_dot(_):
            dve.wait_ge(s_lam, 16)
            for l in range(DEPTH):
                v = lam_in.rearrange("p (l a b d) -> p l a b d", l=DEPTH, a=2, b=2)
                for a in (0, 1):
                    link(nc.vector.tensor_tensor(ta[:, 0:64], v[:, l, a, 0, :], v[:, l, a, 1, :], ALU.mult))
                    link(nc.vector.reduce_sum(lam_sum[:, 2 * l + a:2 * l + a + 1], ta[:, 0:64], AX.X))
            signal(nc.vector.memset(stat[:, :], 0.0), lam_ready, 1)

        def lam_out(_):
            dve.wait_ge(lam_exp, 1)
            for l in range(DEPTH):
                li = lambda_init(l)
                c = slice(l, l + 1)
                link(nc.vector.tensor_tensor(neg_lam[:, c], lam_sum[:, 2 * l + 1:2 * l + 2],
                                             lam_sum[:, 2 * l:2 * l + 1], ALU.subtract))
                link(nc.vector.tensor_scalar(neg_lam[:, c], neg_lam[:, c], -li, None, ALU.add))
                link(nc.vector.tensor_scalar(sub_w[:, c], pcol(l, "sub"), 1.0 - li, None, ALU.mult))

        def x_tile(l, kt):
            n = KT * (l - 1) + kt
            dve.wait_ge(sq_x, 4 + n + 1)
            if kt == 0:
                dve.wait_ge(stat_done, norm_order[("xsum", l - 1)] + 1)
                add = nc.vector.tensor_copy(acc[:, :], sq[:, 0, :])
            else:
                add = nc.vector.tensor_tensor(acc[:, :], acc[:, :], sq[:, kt % 2, :], ALU.add)
            signal(add, acc_ready, 1 + n + 1)
            x_lo(l, kt)

        def x_lo(l, kt):
            n = KT * l + kt
            dve.wait_ge(h_hi_ready, n + 1)
            signal(nc.vector.scalar_tensor_tensor(h_lo[:, kt, :], x[:, kt, :], pcol(l, "norm", kt),
                                                  h_hi[:, kt, :].bitcast(F32), ALU.mult, ALU.subtract),
                   h_ready, n + 1)

        def x_out(l, n):
            t0 = first_query(l)
            for j in (0, 1):
                kt = 2 * n + j
                ps = wait_tile(dve, l, "out", n, j)
                signal(nc.vector.tensor_tensor(x[:, kt, t0:L], x[:, kt, t0:L], ps[:, 0:L - t0], ALU.add),
                       xt_taken, KT * l + kt + 1)
            if l < DEPTH - 1:
                for kt in (2 * n, 2 * n + 1):
                    x_tile(l + 1, kt)

        def split(l, s):
            g = l * SLOTS + s
            e, half = entry(l, s)
            n = chunk_size(s)
            dve.wait_ge(hi_ready, g + 1)
            signal(nc.vector.tensor_tensor(w_lo[:, g % RING, 0:n], raw[:, e % RAW, CHUNK * half:CHUNK * half + n],
                                           w_hi[:, g % RING, 0:n].bitcast(F32), ALU.subtract), lo_ready, g + 1)

        def rescale(l, p, j):
            dve.wait_ge(lifted, scaled_no[(l, p, j)])
            out_ = tile_place(l, p, j)
            dve.wait_ge(rn_ready, norm_order[("xsum", l)] + 1)
            signal(nc.vector.tensor_tensor(out_, out_, rinv[:, tile_from(l, PAIRS[p][0]):L], ALU.mult), scaled,
                   scaled_no[(l, p, j)])

        def rope_fin(l, key, i):
            branch, width = rope[key]
            t0 = rope_from(l, key)
            out_ = rope_target(key, i)[:, t0:L]
            store = {"q": "q", "k": "k"}[key[-1] if key in ("aq", "ak", "bq", "bk") else "q"]
            if branch:
                half = parity("rope_stat", l, key, i)
                dve.wait_ge(stat_done, norm_order[("rope_stat", l, key, i)] + 1)
                cos, sin = const("cos_" + branch)[:, t0:L], const("sin_" + branch)[:, t0:L]
                link(nc.vector.tensor_tensor(ta[:, t0:L], swap_ps[:, t0:L], sin, ALU.mult))
                link(nc.vector.tensor_tensor(tb[:, t0:L], qw[:, half, t0:L], cos, ALU.mult))
                link(nc.vector.tensor_tensor(tb[:, t0:L], tb[:, t0:L], ta[:, t0:L], ALU.add))
                if branch in "ab":
                    free = store_free(l, branch, store, i)
                    if free:
                        dve.wait_ge(scores_ready, free)
            dve.wait_ge(rn_ready, norm_order[("rope_stat", l, key, i)] + 1)
            if branch:
                last = nc.vector.tensor_tensor(out_, tb[:, t0:L], rn[:, t0:L], ALU.mult)
            else:
                last = nc.vector.scalar_tensor_tensor(out_, out_, pcol(l, key), rn[:, t0:L], ALU.mult, ALU.mult)
            signal(last, fin_done, fin_no[("rope_fin", l, key, i)])

        def y_split(*source):
            n, out_, src, _ = y_tile(*source)
            dve.wait_ge(y_hi_done, n)
            signal(nc.vector.tensor_tensor(out_(y_lo), src, out_(y_hi).bitcast(F32), ALU.subtract), y_ready, n)

        def lat_fin(l, key):
            k0, n = LATENT[key]
            dve.wait_ge(rn_ready, norm_order[("lat_stat", l, key)] + 1)
            for k in range(k0, k0 + n):
                ins = nc.vector.scalar_tensor_tensor(c_st[:, k, :], c_st[:, k, :], pcol(l, key, k - k0), rn[:, :],
                                                     ALU.mult, ALU.mult)
                if k < k0 + n - 1:
                    link(ins)
            signal(ins, fin_done, fin_no[("lat_fin", l, key)])

        def sub_fin(l, n):
            h = score_steps(l)[n][2]
            t0 = first_query(l)
            dve.wait_ge(rn_ready, norm_order[("sub_stat", l, n)] + 1)
            signal(nc.vector.scalar_tensor_tensor(ta[:, t0:L], o_ps[:, t0:L], sub_w[:, l:l + 1], rn[:, t0:L],
                                                  ALU.mult, ALU.mult), o_taken, o_before[step_no[(l, n)]] + 1)
            signal(nc.vector.tensor_tensor(yt[:, t0:L], ta[:, t0:L], g_st[:, h, t0:L], ALU.mult), fin_done,
                   fin_no[("sub_fin", l, n)])

        def head_out(l, n):
            _, b, h, i = score_steps(l)[n]
            q, nq = query_tiles(l)[i]
            r = rows_of(b, h)
            k = step_no[(l, n)]
            dve.wait_ge(pv_done, k + 1)
            signal(nc.vector.tensor_tensor(pair_view(yt, nq), pair_view(o_ps, nq), g_st[:, h:h + 2, q:q + nq],
                                           ALU.mult), o_taken, o_before[k] + 1)

        def gate(l, kind, i, j):
            t0 = gate_from(l)
            n = gate_no[("gate", l, kind, i, j)]
            g = row[:, j, 8 + t0:8 + L]
            e = gate_e[:, t0:L]
            dve.wait_ge(gate_exp, n)
            link(nc.vector.tensor_scalar(e, e, 1.0, None, ALU.add))
            link(nc.vector.reciprocal(e, e))
            if kind != "dg":
                signal(nc.vector.tensor_tensor(g_st[:, i, t0:L], g, e, ALU.mult), gate_done, n)
                return
            link(nc.vector.tensor_tensor(ta[:, t0:L], g, e, ALU.mult))
            dve.wait_ge(mixed, 4 * l + i + 1)
            signal(nc.vector.tensor_tensor(yt[:, t0:L], ta[:, t0:L], c_st[:, i, t0:L], ALU.mult), gate_done, n)

        def pool(l, g, j):
            u = row[:, j, :]
            wide = L + 16
            link(nc.vector.tensor_tensor(ta[:, 1:wide], u[:, 0:wide - 1], u[:, 1:wide], ALU.add))
            src, dst, lo, hi, step = ta, tb, 1, wide, 1
            for _ in range(g):
                link(nc.vector.tensor_tensor(dst[:, lo + step:hi - step], src[:, lo:hi - 2 * step],
                                             src[:, lo + 2 * step:hi], ALU.add))
                lo, hi, step = lo + step, hi - step, 2 * step
                src, dst = dst, src
            edge = con[:, CC["edge"] + 16 * g:CC["edge"] + 16 * g + 16]
            link(nc.vector.tensor_tensor(src[:, 8:16], src[:, 8:16], edge[:, 0:8], ALU.mult))
            link(nc.vector.tensor_tensor(src[:, L:L + 8], src[:, L:L + 8], edge[:, 8:16], ALU.mult))
            n = 4 * l + g
            if n:
                dve.wait_ge(mixed_ps, n)
            signal(nc.vector.scalar_tensor_tensor(pooled[:, :], src[:, 8:8 + L], 1.0 / (2 << g), u[:, 8:8 + L],
                                                  ALU.mult, ALU.subtract), pooled_ready, n + 1)

        def s_max(l, n):
            k = step_no[(l, n)]
            _, b, h, i = score_steps(l)[n]
            nq = query_tiles(l)[i][1]
            dve.wait_ge(scores_ready, k + 1)
            for m in (0, 1):
                link(nc.vector.reduce_max(stat[0:nq, m:m + 1], s_ps[m][0:nq, 0:L], AX.X))
            signal(nc.vector.tensor_scalar(stat[0:nq, 2:4], stat[0:nq, 0:2], -SCALE[b], None, ALU.mult),
                   bias_ready, k + 1)

        def s_scale(l, n):
            k = step_no[(l, n)]
            _, b, h, i = score_steps(l)[n]
            nq = query_tiles(l)[i][1]
            dve.wait_ge(exp_done, 2 * k + 2)
            link(nc.vector.reciprocal(stat[0:nq, 6:8], stat[0:nq, 4:6]))
            p = [probs[0:nq, k % 2, m, :] for m in (0, 1)]
            if b == "a":
                link(nc.vector.tensor_tensor(stat[0:nq, 7:8], stat[0:nq, 7:8], neg_lam[0:nq, l:l + 1], ALU.mult))
                link(nc.vector.tensor_scalar(p[1], p[1], stat[0:nq, 7:8], None, ALU.mult))
                last = nc.vector.scalar_tensor_tensor(p[0], p[0], stat[0:nq, 6:7], p[1], ALU.mult, ALU.add)
            else:
                link(nc.vector.tensor_scalar(p[0], p[0], stat[0:nq, 6:7], None, ALU.mult))
                last = nc.vector.tensor_scalar(p[1], p[1], stat[0:nq, 7:8], None, ALU.mult)
            signal(last, w_ready, k + 1)

        run = dict(setup=setup, x_first=x_first, x_add=x_add, lam_dot=lam_dot, lam_out=lam_out,
                   x_out=x_out, split=split, rescale=rescale, rope_fin=rope_fin,
                   lat_fin=lat_fin, sub_fin=sub_fin, head_out=head_out, y_split=y_split, gate=gate, pool=pool,
                   s_max=s_max, s_scale=s_scale)
        waited = [False]
        for stage, *what in vector_plan:
            if stage == "rope_fin" and not waited[0]:
                dve.wait_ge(s_tab, 16)
                waited[0] = True
            if stage in run:
                run[stage](*what)

    ctx.close()


def constants():
    def table(pos, dim, theta):
        inv = np.float32(theta) ** (-np.arange(0, dim, 2, dtype=np.float32) / np.float32(dim))
        ang = (pos.astype(np.float32)[:, None] * inv[None, :].astype(np.float32)).astype(np.float32)
        c, s = np.cos(ang.astype(np.float64)).T, np.sin(ang.astype(np.float64)).T
        return np.concatenate([c, c]), np.concatenate([-s, s])

    out = np.zeros((128, N_CONST), np.float32)

    def put(name, a):
        out[:, CC[name]:CC[name] + a.shape[1]] = a

    pos = np.arange(L)
    rot = 16
    c, s = table(pos, rot, 500000.0)
    cos_a, sin_a = np.ones((128, L)), np.zeros((128, L))
    for m in (0, 64):
        cos_a[m:m + rot], sin_a[m:m + rot] = c, s
    put("cos_a", cos_a)
    put("sin_a", sin_a)
    rows = np.concatenate([np.full(N_META, -1), np.repeat(np.arange(SEQ // GRID_W), GRID_W)])
    cols = np.concatenate([np.arange(N_META), np.tile(np.arange(GRID_W), SEQ // GRID_W)])
    (cr, sr), (cc, sc) = table(rows, 64, 10000.0), table(cols, 64, 10000.0)
    put("cos_b", np.concatenate([cr, cc]))
    put("sin_b", np.concatenate([sr, sc]))
    c, s = table(pos, 64, 500000.0)
    put("cos_c", np.concatenate([c, c]))
    put("sin_c", np.concatenate([s, s]))
    i = np.arange(128)
    put("ident", np.eye(128))
    put("ones", np.ones((128, 128)))
    put("halves", (i[:, None] // 64 == i[None, :] // 64).astype(np.float32))
    put("swap8", ((i[:, None] ^ 8) == i[None, :]).astype(np.float32))
    put("swap32", ((i[:, None] ^ 32) == i[None, :]).astype(np.float32))
    t = np.concatenate([np.arange(8), np.arange(L - 8, L)])
    for g in range(4):
        w = 2 << g
        n = np.clip(t + w - w // 2, 0, L) - np.clip(t - w // 2, 0, L)
        out[:, CC["edge"] + 16 * g:CC["edge"] + 16 * g + 16] = w / n.astype(np.float64)
    return out


def pack_weights(w_in, w_out, uq, ukv):
    stream = np.zeros((DEPTH * ENTRIES, 128, 2, CHUNK), w_in.dtype)
    for l in range(DEPTH):
        wi = w_in[l].reshape(KT, 128, -1)
        wo = w_out[l].reshape(KT, 128, -1)
        n = l * 2 * ENTRIES

        def add(block):
            nonlocal n
            b = block.transpose(1, 0, 2).reshape(128, -1)
            stream[n // 2, :, n % 2, :b.shape[1]] = b
            n += 1

        for p in range(N_PAIRS):
            kind, i = PAIRS[p]
            if kind == "cqr":
                a, r = OFF["cq"] + 256, OFF["ckr"]
                cols = np.concatenate([wi[:, :, a:a + 128], wi[:, :, r:r + 64], wi[:, :, r:r + 64]], axis=2)
            else:
                a = OFF[kind] + 128 * i
                cols = wi[:, :, a:a + 256]
            for b in range(KT // CK):
                add(cols[CK * b:CK * b + CK])
            if p == LEAD_PAIRS - 1:
                q = uq[l].reshape(3, 128, 4, 192)
                kv = ukv[l].reshape(2, 128, 4, 256)
                add(q[:, :, 0:2, 0:128].reshape(3, 128, 256))
                add(q[:, :, 2:4, 0:128].reshape(3, 128, 256))
                add(q[:, :, :, 128:].reshape(3, 128, 256))
                add(kv[:, :, :, 0:128].reshape(2, 128, 512))
                add(kv[:, :, :, 128:].reshape(2, 128, 512))
                n += 1
        for p in range(O_PAIRS):
            for b in range(KT // CK):
                k = CK * OUT_ORDER[b]
                add(wo[k:k + CK, :, 256 * p:256 * p + 256])
    return stream.reshape(DEPTH * ENTRIES, 128, 2 * CHUNK)


def pack_params(v):
    par = np.zeros((128, DEPTH, N_PAR), np.float32)

    def put(name, a):
        a = a.reshape(DEPTH, -1, 128).transpose(2, 0, 1)
        par[:, :, PC[name]:PC[name] + a.shape[2]] = a

    twice = lambda a: np.concatenate([a, a], axis=1)
    put("norm", v["norm_w"])
    put("aq", twice(v["a_q_norm"]))
    put("ak", twice(v["a_k_norm"]))
    put("sub", v["a_subln"])
    put("bq", v["b_q_norm"])
    put("bk", v["b_k_norm"])
    put("cq", v["c_q_lat_norm"])
    put("ckv", v["c_kv_lat_norm"])
    put("qn", v["c_q_norm"][:, :128])
    put("qr", twice(v["c_q_norm"][:, 128:]))
    put("kn", v["c_k_norm"][:, :128])
    put("kr", twice(v["c_k_norm"][:, 128:]))
    put("dsc", v["d_scale"])
    return par.reshape(128, DEPTH * N_PAR)


def kernel(**inputs):
    import concourse.bacc as _bacc
    from concourse.bass_utils import run_bass_kernel_spmd as _run

    v = {k: np.asarray(a) for k, a in inputs.items()}
    tokens = np.concatenate([v["meta_tokens"], v["x"][0]], axis=0)
    d_w = v["d_w_group"].transpose(2, 0, 1, 3).reshape(128, -1)
    arrays = {
        "xt": np.ascontiguousarray(tokens.reshape(L, KT, 128).transpose(2, 1, 0)),
        "w_stream": pack_weights(v["w_in"], v["w_out"], v["c_w_uq"], v["c_w_ukv"]),
        "params": pack_params(v),
        "lam_rows": np.ascontiguousarray(np.broadcast_to(v["a_lambda"].reshape(1, -1), (128, DEPTH * 256))),
        "consts": np.concatenate([constants(), d_w], axis=1),
    }
    nc = _bacc.Bacc("TRN2", target_bir_lowering=False, num_devices=1)
    args = [nc.dram_tensor(f"{n}_dram", a.shape, mybir.dt.from_np(a.dtype), kind="ExternalInput").ap()
            for n, a in arrays.items()]
    out = nc.dram_tensor("out_dram", (128, KT, SEQ), mybir.dt.float32, kind="ExternalOutput").ap()
    build(nc, *args, out)
    r = _run(nc, [{f"{n}_dram": a for n, a in arrays.items()}], core_ids=[0])
    got = r.results[0]["out_dram"]
    return np.ascontiguousarray(got.transpose(2, 1, 0)).reshape(1, SEQ, D_MODEL)
```
